# Optimizing a Trainium2 kernel written in Bass

```python
import math
import jax, jax.numpy as jnp
from jax import lax
import numpy as np

D_MODEL = 1024
BATCH = 1
SEQ = 4096
DEPTH = 1
DEC_BATCH = 1
DEC_SEQ = 2048
PAST_LEN = 128

HEAD_DIM = 64
N_ATTN_HEADS = 12
D_ATTN = N_ATTN_HEADS * HEAD_DIM
N_FOURIER_GROUPS = 4
FOURIER_GROUP = 64
D_FOURIER = N_FOURIER_GROUPS * FOURIER_GROUP
D_MIX = D_ATTN + D_FOURIER
D_IN_PROJ = 4 * D_ATTN + 2 * D_FOURIER
PATTERNS = ((128, 1), (512, 4), (2048, 16))
BLOCK = 64
N_BUCKETS = 32
MAX_DISTANCE = 1024
RMS_EPS = 1e-6
NEG = -1e30

kernel_name = "hybrid_dilated_attn_fnet_encoder"

def rmsnorm(x, g):
    xf = x.astype(jnp.float32)
    y = xf * lax.rsqrt(jnp.mean(xf * xf, axis=-1, keepdims=True) + RMS_EPS) * g.astype(jnp.float32)
    return y.astype(x.dtype)

def t5_bucket(rel):
    half = N_BUCKETS // 2
    max_exact = half // 2
    ret = jnp.where(rel > 0, half, 0)
    n = jnp.abs(rel)
    nf = jnp.maximum(n, 1).astype(jnp.float32)
    large = max_exact + (jnp.log(nf / max_exact) / math.log(MAX_DISTANCE / max_exact)
                         * (half - max_exact)).astype(jnp.int32)
    large = jnp.minimum(large, half - 1)
    return ret + jnp.where(n < max_exact, n, large)

def dilated_window_attention(q, k, v, rel_bias, window, dil):
    B, S, H, Dh = q.shape
    half = window // (2 * dil)
    L = S // dil
    nb = -(-L // BLOCK)
    Lp = nb * BLOCK

    def to_residue(t):
        return t.reshape(B, L, dil, H, Dh).transpose(0, 2, 1, 3, 4)

    qr, kr, vr = to_residue(q), to_residue(k), to_residue(v)
    qb = jnp.pad(qr, ((0, 0), (0, 0), (0, Lp - L), (0, 0), (0, 0))).reshape(B, dil, nb, BLOCK, H, Dh)

    def key_blocks(t):
        tp = jnp.pad(t, ((0, 0), (0, 0), (BLOCK, Lp - L + BLOCK), (0, 0), (0, 0)))
        tp = tp.reshape(B, dil, nb + 2, BLOCK, H, Dh)
        return jnp.concatenate([tp[:, :, 0:nb], tp[:, :, 1:nb + 1], tp[:, :, 2:nb + 2]], axis=3)

    kb, vb = key_blocks(kr), key_blocks(vr)

    a = jnp.arange(BLOCK, dtype=jnp.int32)[:, None]
    c = jnp.arange(3 * BLOCK, dtype=jnp.int32)[None, :]
    rel = c - BLOCK - a
    band = jnp.abs(rel) <= half
    key_pos = jnp.arange(nb, dtype=jnp.int32)[:, None] * BLOCK + jnp.arange(3 * BLOCK, dtype=jnp.int32)[None, :] - BLOCK
    in_range = (key_pos >= 0) & (key_pos < L)
    mask = band[None] & in_range[:, None, :]
    bias = rel_bias[t5_bucket(rel * dil)].astype(jnp.float32).transpose(2, 0, 1)

    scale = 1.0 / math.sqrt(Dh)
    s = jnp.einsum('brnqhd,brnkhd->brnhqk', qb, kb, preferred_element_type=jnp.float32) * scale + bias
    s = jnp.where(mask[:, None], s, NEG)
    lse = jax.nn.logsumexp(s, axis=-1)
    p = jnp.exp(s - lse[..., None])
    o = jnp.einsum('brnhqk,brnkhd->brnqhd', p.astype(vb.dtype), vb, preferred_element_type=jnp.float32)
    o = o.reshape(B, dil, Lp, H, Dh)[:, :, :L].transpose(0, 2, 1, 3, 4).reshape(B, S, H, Dh)
    lse = lse.transpose(0, 1, 2, 4, 3).reshape(B, dil, Lp, H)[:, :, :L].transpose(0, 2, 1, 3).reshape(B, S, H)
    return o, lse

def encoder_layer(x, norm_g, w_in, q_g, k_g, rel_bias, w_four, w_out):
    B, S, _ = x.shape
    h = rmsnorm(x, norm_g)
    proj = h @ w_in
    q, k, v, g_attn, u, g_four = jnp.split(
        proj, [D_ATTN, 2 * D_ATTN, 3 * D_ATTN, 4 * D_ATTN, 4 * D_ATTN + D_FOURIER], axis=-1)

    q = rmsnorm(q.reshape(B, S, N_ATTN_HEADS, HEAD_DIM), q_g)
    k = rmsnorm(k.reshape(B, S, N_ATTN_HEADS, HEAD_DIM), k_g)
    v = v.reshape(B, S, N_ATTN_HEADS, HEAD_DIM)
    outs, lses = [], []
    for window, dil in PATTERNS:
        o, l = dilated_window_attention(q, k, v, rel_bias, window, dil)
        outs.append(o)
        lses.append(l)
    wts = jax.nn.softmax(jnp.stack(lses), axis=0)
    attn = jnp.einsum('pbsh,pbshd->bshd', wts, jnp.stack(outs))
    attn = attn.reshape(B, S, D_ATTN).astype(x.dtype) * jax.nn.silu(g_attn)

    uf = u.astype(jnp.float32).reshape(B, S, N_FOURIER_GROUPS, FOURIER_GROUP)
    mixed = jnp.fft.fftn(uf, axes=(1, 3), norm="ortho").real
    four = jnp.einsum('bsgc,gce->bsge', mixed.astype(x.dtype), w_four).reshape(B, S, D_FOURIER)
    four = four * jax.nn.silu(g_four)

    y = jnp.concatenate([attn, four], axis=-1) @ w_out
    return x + y

def setup_inputs(seed: int = 0) -> dict:
    key = jax.random.key(seed)
    ks = jax.random.split(key, 10)
    f32 = jnp.float32
    x_prompt = jax.random.normal(ks[0], (BATCH, SEQ, D_MODEL), f32)
    x_sample = jax.random.normal(ks[1], (DEC_BATCH, DEC_SEQ, D_MODEL), f32)
    norm_g = 1.0 + 0.01 * jax.random.normal(ks[2], (DEPTH, D_MODEL), f32)
    w_in = jax.random.normal(ks[3], (DEPTH, D_MODEL, D_IN_PROJ), f32) * D_MODEL ** -0.5
    q_norm_g = 1.0 + 0.01 * jax.random.normal(ks[4], (DEPTH, HEAD_DIM), f32)
    k_norm_g = 1.0 + 0.01 * jax.random.normal(ks[5], (DEPTH, HEAD_DIM), f32)
    rel_bias = 0.1 * jax.random.normal(ks[6], (N_BUCKETS, N_ATTN_HEADS), f32)
    w_four = jax.random.normal(ks[7], (DEPTH, N_FOURIER_GROUPS, FOURIER_GROUP, FOURIER_GROUP), f32) * FOURIER_GROUP ** -0.5
    w_out = jax.random.normal(ks[8], (DEPTH, D_MIX, D_MODEL), f32) * D_MIX ** -0.5
    return {"x_prompt": x_prompt, "x_sample": x_sample, "norm_g": norm_g, "w_in": w_in,
            "q_norm_g": q_norm_g, "k_norm_g": k_norm_g, "rel_bias": rel_bias,
            "w_four": w_four, "w_out": w_out}

def reference(x_prompt, x_sample, norm_g, w_in, q_norm_g, k_norm_g, rel_bias, w_four, w_out):
    y_prompt = x_prompt
    y_sample = x_sample
    for layer in range(DEPTH):
        y_prompt = encoder_layer(y_prompt, norm_g[layer], w_in[layer], q_norm_g[layer], k_norm_g[layer],
                                 rel_bias, w_four[layer], w_out[layer])
        y_sample = encoder_layer(y_sample, norm_g[layer], w_in[layer], q_norm_g[layer], k_norm_g[layer],
                                 rel_bias, w_four[layer], w_out[layer])
    return (y_prompt, y_sample)


_drawn_inputs = setup_inputs


def setup_inputs(seed=0):
    import zlib

    import numpy as np

    out = dict(_drawn_inputs(seed))
    spreads = {}
    factors = {'norm_g': 8.0, 'q_norm_g': 8.0, 'k_norm_g': 8.0, 'rel_bias': 8.0}
    for name, (base, spread) in spreads.items():
        noise = np.random.default_rng([zlib.crc32(name.encode()), seed]).standard_normal(out[name].shape)
        drawn = base * np.exp(spread * noise) if base else spread * noise
        out[name] = __import__('jax').numpy.asarray(drawn.astype(out[name].dtype))
    for name, factor in factors.items():
        out[name] = (out[name] * factor).astype(out[name].dtype)
    return out
```

```python
import math
from contextlib import ExitStack

import numpy as np

import concourse.bass as bass
from concourse import mybir
from concourse.alu_op_type import AluOpType as ALU

F32 = mybir.dt.float32
F32R = mybir.dt.float32r
ACT = mybir.ActivationFunctionType
AX = mybir.AxisListType

P = 128
D = 1024
HD = 64
NH = 12
DA = NH * HD
NG = 4
DF = NG * HD
SEQS = (4096, 2048)
BASES = (0, 4096)
TOKENS = sum(SEQS)
TILES = TOKENS // P
KC = D // P
HALF = 2 * DA + DF
BANK = 512
BUCKETS = 32
MAX_DISTANCE = 1024
EPS = 1e-6
NEG = -1e30
DILS = (1, 4, 16)
REACH = 64
LINE = 384
VW = HD + 1
VROW = (NH + 1) * VW
OROW = NH * VW + NH
PAIRS = NH // 2
N2 = 64



def t5_bucket(rel):
    half = BUCKETS // 2
    exact = half // 2
    n = np.abs(rel)
    nf = np.maximum(n, 1).astype(np.float32)
    large = exact + (np.log(nf / np.float32(exact)) / np.float32(math.log(MAX_DISTANCE / exact))
                     * np.float32(half - exact)).astype(np.int32)
    return np.where(rel > 0, half, 0) + np.where(n < exact, n, np.minimum(large, half - 1))


def constants():
    rel = np.arange(LINE) - (LINE // 2 - 1)
    onehot = np.zeros((BUCKETS + 1, len(DILS) * LINE), np.float32)
    for i, dil in enumerate(DILS):
        for j, r in enumerate(rel):
            row = t5_bucket(np.asarray(r * dil)) if abs(r) <= REACH else BUCKETS
            onehot[row, i * LINE + j] = 1.0 if abs(r) <= REACH else NEG
    a = 2 * np.pi * np.outer(np.arange(HD), np.arange(HD)) / HD
    two = np.eye(2)
    chan = np.concatenate([np.kron(two, np.cos(a)), np.kron(two, np.sin(a))], axis=1)
    out = {"c_ident": np.eye(P), "c_onehot": onehot, "c_chan": chan}
    for name, s in zip("ab", SEQS):
        n1 = s // N2
        a = 2 * np.pi * np.outer(np.arange(n1), np.arange(n1)) / n1
        c, sn = np.cos(a), np.sin(a)
        out["c_first_" + name] = np.block([[c, -sn], [-sn, -c]])
        n, k1, k2 = np.arange(N2)[:, None, None], np.arange(n1)[None, :, None], np.arange(N2)[None, None, :]
        a = 2 * np.pi * ((n * (k1 + n1 * k2)) % s) / s
        second = np.concatenate([np.cos(a), np.sin(a)], axis=0) / math.sqrt(s * HD)
        out["c_second_" + name] = second.reshape(2 * N2, n1 * N2)
    return {k: np.ascontiguousarray(v, np.float32) for k, v in out.items()}


class Core:

    def __init__(self, nc, io):
        self.nc, self.io, self.keep = nc, io, ExitStack()

    def sb(self, stack, name, shape, dt=F32):
        return stack.enter_context(self.nc.sbuf_tensor(name, shape, dt))

    def ps(self, stack, name):
        return stack.enter_context(self.nc.psum_tensor(name, [P, BANK], F32))

    def sem(self, name):
        return self.keep.enter_context(self.nc.semaphore(name))


def build(nc, io):
    core = Core(nc, io)
    with core.keep:
        core.ident = core.sb(core.keep, "ident", [P, P])
        core.rstd_x = core.sb(core.keep, "rstd_x", [P, TILES])
        scratch = {"q": [TOKENS, DA], "k": [TOKENS, DA], "v": [TOKENS, VROW], "gate": [TOKENS, D],
                   "ab": [TOKENS, 2 * DF], "four": [TOKENS, DF], "line": [len(DILS), NH, P, LINE],
                   "o": [len(DILS), TOKENS, OROW],
                   "g_a": [2 * SEQS[0] // N2, N2 * DF], "g_b": [2 * SEQS[1] // N2, N2 * DF]}
        core.dram = {k: nc.dram_tensor("scratch_" + k, s, F32, kind="Internal").ap() for k, s in scratch.items()}
        with ExitStack() as tables:
            core.chan_w = core.sb(tables, "chan_w", [P, 2, 2 * P])
            setup(core)
            project(core, 0)
            project(core, 1)
        for name, seq, base in zip("ab", SEQS, BASES):
            fourier(core, name, seq, base)
        attention(core)
        combine(core)



def setup(core):
    nc, io, dram = core.nc, core.io, core.dram
    loaded, cleared, mm_done, line_out, stored = (core.sem("setup_" + n) for n in
                                                  ("loaded", "cleared", "mm_done", "copied", "stored"))
    with ExitStack() as st:
        onehot = core.sb(st, "onehot", [BUCKETS + 1, len(DILS) * LINE])
        rel = core.sb(st, "rel", [BUCKETS + 1, NH])
        line = core.sb(st, "line", [NH, len(DILS) * LINE])
        chan = core.sb(st, "chan", [P, 2 * P])
        wf = core.sb(st, "wf", [P, 2, P])
        ps_line = [core.ps(st, f"ps_line{i}") for i in range(len(DILS))]
        ps_chan = [core.ps(st, f"ps_chan{i}") for i in range(2)]
        block = st.enter_context(nc.Block())
        n_loads = 4 + NG

        @block.gpsimd
        def _(pool):
            pool.memset(wf[:], 0.0).then_inc(cleared, 1)
            pool.memset(rel[:], 1.0).then_inc(cleared, 1)

        @block.sync
        def _(sp):
            sp.dma_start(core.ident[:], io["c_ident"]).then_inc(loaded, 16)
            sp.dma_start(onehot[:], io["c_onehot"]).then_inc(loaded, 16)
            sp.dma_start(chan[:], io["c_chan"]).then_inc(loaded, 16)
            sp.wait_ge(cleared, 2)
            sp.dma_start(rel[0:BUCKETS, :], io["rel_bias"]).then_inc(loaded, 16)
            for g in range(NG):
                lo = HD * (g % 2)
                sp.dma_start(wf[lo:lo + HD, g // 2, lo:lo + HD], io["w_four"][g]).then_inc(loaded, 16)
            sp.wait_ge(line_out, 1)
            for i in range(len(DILS)):
                sp.dma_start(dram["line"][i], line[:, i * LINE:(i + 1) * LINE].rearrange("h (a j) -> h a j", a=1)
                             .broadcast_to([NH, P, LINE])).then_inc(stored, 16)
            sp.wait_ge(stored, 16 * len(DILS))

        @block.tensor
        def _(pe):
            pe.wait_ge(loaded, 16 * n_loads)
            for i in range(len(DILS)):
                pe.matmul(ps_line[i][0:NH, 0:LINE], rel[:], onehot[:, i * LINE:(i + 1) * LINE],
                          start=True, stop=True).then_inc(mm_done, 1)
            for gp in range(2):
                for ab in range(2):
                    pe.matmul(ps_chan[gp][:, ab * P:(ab + 1) * P], chan[:, ab * P:(ab + 1) * P], wf[:, gp, :],
                              start=True, stop=True).then_inc(mm_done, 1)

        @block.vector
        def _(dve):
            dve.wait_ge(mm_done, len(DILS) + 2 * 2)
            for i in range(len(DILS)):
                last = dve.tensor_copy(line[:, i * LINE:(i + 1) * LINE], ps_line[i][0:NH, 0:LINE])
            last.then_inc(line_out, 1)
            for gp in range(2):
                dve.tensor_copy(core.chan_w[:, gp, :], ps_chan[gp][:, 0:2 * P])



def project(core, half):
    nc, io, dram = core.nc, core.io, core.dram
    name = lambda n: f"p{half}_{n}"
    S = lambda n: core.sem(name(n))
    w_in, w_hi_done, w_lo_done = [S("w_in0"), S("w_in1")], S("w_hi_done"), S("w_lo_done")
    gain_in, x_in, ones_done = S("gain_in"), [S("x_in0"), S("x_in1")], S("ones_done")
    sq_done, root_done, mean_done, h_done = S("sq_done"), S("root_done"), S("mean_done"), S("h_done")
    t_done, hi_done, lo_done = S("t_done"), S("hi_done"), S("lo_done")
    mm_done = [S(f"mm_done{c}") for c in range(4)]
    out_done = [S(f"out_done{c}") for c in range(4)]
    expo_done, chain = S("expo_done"), S("chain")
    v_tail_done = S("v_tail_done")
    u_done, ut_done, ut_copied, ab_done = S("u_done"), S("ut_done"), S("ut_copied"), S("ab_done")
    stored = [S("stored0"), S("stored1")]
    n_stores = 3 if half == 0 else 2
    order = (3, 0, 1, 2)
    width = [BANK, BANK, BANK, HALF - 3 * BANK]
    source = [half * 2 * DA + c * BANK for c in range(3)] + [4 * DA + half * DF]
    units = [(c, slice(k, k + KC // 2)) for c in order for k in (0, KC // 2)]

    first = lambda t: isinstance(t, int) and t == 0
    early = lambda t: isinstance(t, int) and t < 2
    late = lambda t: isinstance(t, int) and t >= TILES - 2
    last = lambda t: isinstance(t, int) and t == TILES - 1
    x_loads = lambda t, s: (t - s) * 8 + 16
    slot_stores = lambda t, s: (t - s) * (8 * n_stores)
    norm_x_nr = lambda t: t + 1 if early(t) else t * 4 - 3
    norm_c_nr = lambda t, c: t * 4 + (c + 3 if c < 2 or late(t) else c + 4) - (1 if last(t) else 0)
    X_LINKS, C_LINKS = 5, 6
    TILE_LINKS = X_LINKS + 3 * C_LINKS

    def tiles(engine, step):
        step(0, 0)
        step(1, 1)
        with engine.Fori(1, TILES // 2 - 1) as it:
            step(it * 2, 0)
            step(it * 2 + 1, 1)
        step(TILES - 2, 0)
        step(TILES - 1, 1)

    with ExitStack() as st:
        sb = lambda n, shape, dt=F32: core.sb(st, name(n), shape, dt)
        w_hi, w_lo = sb("w_hi", [P, KC, HALF], F32R), sb("w_lo", [P, KC, HALF], F32R)
        stage = [sb(f"stage{i}", [P, KC // 2, BANK]) for i in range(2)]
        gain = sb("gain", [P, KC])
        x = [sb(f"x{i}", [P, D]) for i in range(2)]
        h = [sb(f"h{i}", [P, D]) for i in range(2)]
        h_hi = [sb(f"h_hi{i}", [P, KC, P], F32R) for i in range(2)]
        h_lo = [sb(f"h_lo{i}", [P, KC, P], F32R) for i in range(2)]
        if half == 0:
            squares_x, sumsq_x = sb("squares_x", [P, D]), sb("sumsq_x", [P, 1])
            squares = sb("squares", [P, BANK])
            sumsq, mean, root, inv, work, rstd = (sb(n, [P, 8]) for n in
                                                  ("sumsq", "mean", "root", "inv", "work", "rstd"))
            rows = [sb(f"qk{i}", [P, 2 * DA]) for i in range(2)]
            ab = [sb(f"ab{i}", [P, 2 * DF]) for i in range(2)]
            u, ut = sb("u", [P, DF]), sb("ut", [P, 2 * P])
        else:
            rows = [sb(f"v{i}", [P, VROW]) for i in range(2)]
            gate = [sb(f"gate{i}", [P, D]) for i in range(2)]
            expo, denom = sb("expo", [P, BANK]), sb("denom", [P, BANK])
        ps = [core.ps(st, name(f"ps{c}")) for c in range(4)]
        ps_t = [core.ps(st, name(f"ps_t{c}")) for c in range(4)]
        block = st.enter_context(nc.Block())

        @block.gpsimd
        def _(pool):
            if half == 1:
                for i in range(2):
                    pool.memset(rows[i][:], 1.0).then_inc(ones_done, 1)

        @block.sync
        def _(sp):
            def load_x(t, s):
                if not early(t):
                    sp.wait_ge(h_done, t - 1)
                sp.dma_start(x[s][:], io["x"][bass.ds(t * P, P), :]).then_inc(x_in[s], 16)

            with nc.allow_non_contiguous_dma(reason="a gain per channel, 4 KiB in all"):
                sp.dma_start(gain[:], io["norm_g"].rearrange("(k p) -> p k", p=P)).then_inc(gain_in, 16)
            load_x(0, 0)
            w_rows = io["w_in"].rearrange("(k p) n -> p k n", p=P)
            for n, (c, ks) in enumerate(units):
                if n >= 2:
                    sp.wait_ge(w_lo_done, n - 1)
                sp.dma_start(stage[n % 2][:, :, 0:width[c]],
                             w_rows[:, ks, source[c]:source[c] + width[c]]).then_inc(w_in[n % 2], 16)
                if n == 1:
                    load_x(1, 1)

            def step(t, s):
                if not late(t):
                    load_x(t + 2, s)
                for c in range(4):
                    sp.wait_ge(out_done[c], t + 1)
                to = bass.ds(t * P, P)
                if half == 0:
                    sp.dma_start(dram["q"][to, :], rows[s][:, 0:DA]).then_inc(stored[s], 16)
                    sp.dma_start(dram["k"][to, :], rows[s][:, DA:2 * DA]).then_inc(stored[s], 16)
                    sp.dma_start(dram["ab"][to, :], ab[s][:]).then_inc(stored[s], 16)
                else:
                    sp.dma_start(dram["v"][to, :], rows[s][:]).then_inc(stored[s], 16)
                    sp.dma_start(dram["gate"][to, :], gate[s][:]).then_inc(stored[s], 16)

            tiles(sp, step)
            for s in range(2):
                sp.wait_ge(stored[s], 16 * n_stores * (TILES // 2))

        @block.tensor
        def _(pe):
            def turn(t, s):
                pe.wait_ge(h_done, t + 1)
                if not early(t):
                    pe.wait_ge(lo_done, t * 2 - 2)
                for j in range(2):
                    for k in range(4):
                        ins = pe.transpose(ps_t[2 * s + j][:, k * P:(k + 1) * P],
                                           h[s][:, (4 * j + k) * P:(4 * j + k + 1) * P], core.ident[:])
                    ins.then_inc(t_done, 1)

            def product(t, s, c):
                if not first(t):
                    pe.wait_ge(out_done[c], t)
                else:
                    pe.wait_ge(w_lo_done, 2 * order.index(c) + 2)
                cols = slice(c * BANK, c * BANK + width[c])
                for k in range(KC):
                    for n, (a, b) in enumerate(((h_hi, w_hi), (h_hi, w_lo), (h_lo, w_hi))):
                        ins = pe.matmul(ps[c][:, 0:width[c]], a[s][:, k, :], b[:, k, cols],
                                        start=(k == 0 and n == 0), stop=(k == KC - 1 and n == 2))
                ins.then_inc(mm_done[c], 1)

            def turn_u(t):
                pe.wait_ge(u_done, t + 1)
                for j in range(2):
                    ins = pe.transpose(ps[3][:, DF + j * P:DF + (j + 1) * P], u[:, j * P:(j + 1) * P], core.ident[:])
                ins.then_inc(ut_done, 1)

            def channel_dft(t):
                pe.wait_ge(ut_copied, t + 1)
                to = ps[3][:].rearrange("p (ab j c) -> p ab j c", ab=2, j=2)
                for j in range(2):
                    ins = pe.matmul(to[:, :, j, :], ut[:, j * P:(j + 1) * P],
                                    core.chan_w[:, j, :].rearrange("p (ab c) -> p ab c", ab=2),
                                    start=True, stop=True)
                ins.then_inc(ab_done, 1)

            def step(t, s):
                pe.wait_ge(lo_done, t * 2 + 2)
                for n, c in enumerate(order):
                    product(t, s, c)
                    if n == 0 and not last(t):
                        turn(t + 1, 1 - s)
                    if half == 0 and n == 1:
                        turn_u(t)
                    if half == 0 and n == 2:
                        channel_dft(t)

            turn(0, 0)
            tiles(pe, step)

        @block.scalar
        def _(act):
            def norm_x(t, s):
                act.wait_ge(x_in[s], x_loads(t, s))
                act.activation(squares_x[:], x[s][:], ACT.Square, accum_out=sumsq_x[:, 0:1]).then_inc(sq_done, 1)
                act.wait_ge(mean_done, norm_x_nr(t))
                act.activation(root[:, 0:1], mean[:, 0:1], ACT.Sqrt).then_inc(root_done, 1)

            def split(t, s):
                for j in range(2):
                    act.wait_ge(t_done, t * 2 + j + 1)
                    if j == 0 and not early(t):
                        act.wait_ge(mm_done[order[-1]], t - 1)
                    for k in range(4):
                        ins = act.activation(h_hi[s][:, 4 * j + k, :], ps_t[2 * s + j][:, k * P:(k + 1) * P],
                                             ACT.Copy, scale=gain[:, 4 * j + k:4 * j + k + 1])
                    ins.then_inc(hi_done, 1)

            def head_squares(t, c):
                act.wait_ge(mm_done[c], t + 1)
                act.activation(squares[:], ps[c][:], ACT.Square).then_inc(sq_done, 1)
                act.wait_ge(mean_done, norm_c_nr(t, c))
                act.activation(root[:], mean[:], ACT.Sqrt).then_inc(root_done, 1)

            def values(t, s, c):
                if c == 0 and not early(t):
                    act.wait_ge(stored[s], slot_stores(t, s))
                n = 8 if c == 0 else 4
                act.activation(rows[s][:, 0:NH * VW].rearrange("p (h w) -> p h w", w=VW)[:, 8 * c:8 * c + n, 0:HD],
                               ps[c][:, 0:n * HD].rearrange("p (h w) -> p h w", w=HD),
                               ACT.Copy).then_inc(out_done[0] if c == 0 else v_tail_done, 1)

            def gate_exp(t, c):
                lo = 4 * HD if c == 1 else 0
                before = {3: 2, 1: 3, 2: 1}[c]
                if not (first(t) and c == 3):
                    act.wait_ge(out_done[before], t if c == 3 else t + 1)
                act.activation(expo[:, lo:width[c]], ps[c][:, lo:width[c]], ACT.Exp,
                               scale=-1.0).then_inc(expo_done, 1)

            def step(t, s):
                if not last(t):
                    split(t + 1, 1 - s)
                if half == 0:
                    for c in range(3):
                        if c == 2 and not late(t):
                            norm_x(t + 2, s)
                        head_squares(t, c)
                else:
                    for c in order:
                        act.wait_ge(mm_done[c], t + 1)
                        if c < 2:
                            values(t, s, c)
                        if c > 0:
                            gate_exp(t, c)

            def split_w(n):
                c, ks = units[n]
                act.wait_ge(w_in[n % 2], 16 * (n // 2 + 1))
                act.activation(w_hi[:, ks, c * BANK:c * BANK + width[c]], stage[n % 2][:, :, 0:width[c]],
                               ACT.Copy).then_inc(w_hi_done, 1)

            act.wait_ge(gain_in, 16)
            if half == 0:
                norm_x(0, 0)
            else:
                act.wait_ge(ones_done, 2)
            split(0, 0)
            for n in range(len(units)):
                split_w(n)
            if half == 0:
                norm_x(1, 1)
            tiles(act, step)

        @block.vector
        def _(dve):
            def rsqrt(out, n, roots, links):
                dve.wait_ge(root_done, roots)
                dve.reciprocal(inv[:, 0:n], root[:, 0:n]).then_inc(chain, 1)
                dve.wait_ge(chain, links + 1)
                dve.tensor_tensor(work[:, 0:n], inv[:, 0:n], inv[:, 0:n], ALU.mult).then_inc(chain, 1)
                dve.wait_ge(chain, links + 2)
                dve.tensor_tensor(work[:, 0:n], work[:, 0:n], mean[:, 0:n], ALU.mult).then_inc(chain, 1)
                dve.wait_ge(chain, links + 3)
                dve.tensor_scalar(work[:, 0:n], work[:, 0:n], -0.5, 1.5, ALU.mult, ALU.add).then_inc(chain, 1)
                dve.wait_ge(chain, links + 4)
                dve.tensor_tensor(out, inv[:, 0:n], work[:, 0:n], ALU.mult).then_inc(chain, 1)
                dve.wait_ge(chain, links + 5)

            def norm_x(t, s, links):
                kept = core.rstd_x[:, bass.ds(t, 1)]
                if half == 0:
                    dve.wait_ge(sq_done, norm_x_nr(t))
                    dve.tensor_scalar(mean[:, 0:1], sumsq_x[:, 0:1], 1.0 / D, EPS, ALU.mult,
                                      ALU.add).then_inc(mean_done, 1)
                    rsqrt(kept, 1, norm_x_nr(t), links)
                else:
                    dve.wait_ge(x_in[s], x_loads(t, s))
                if not early(t):
                    dve.wait_ge(t_done, t * 2 - 2)
                dve.tensor_scalar(h[s][:], x[s][:], kept, None, ALU.mult).then_inc(h_done, 1)

            def split(t, s):
                for j in range(2):
                    dve.wait_ge(hi_done, t * 2 + j + 1)
                    for k in range(4):
                        kk = 4 * j + k
                        ins = dve.scalar_tensor_tensor(h_lo[s][:, kk, :], ps_t[2 * s + j][:, k * P:(k + 1) * P],
                                                       gain[:, kk:kk + 1], h_hi[s][:, kk, :].bitcast(F32),
                                                       ALU.mult, ALU.subtract)
                    ins.then_inc(lo_done, 1)

            def slot_free(t, s):
                if not early(t):
                    dve.wait_ge(stored[s], slot_stores(t, s))

            def head_norm(t, s, c, links):
                dve.wait_ge(sq_done, norm_c_nr(t, c))
                dve.tensor_reduce(sumsq[:], squares[:].rearrange("p (h w) -> p h w", w=HD), AX.X,
                                  ALU.add).then_inc(chain, 1)
                dve.wait_ge(chain, links + 1)
                dve.tensor_scalar(mean[:], sumsq[:], 1.0 / HD, EPS, ALU.mult, ALU.add).then_inc(mean_done, 1)
                rsqrt(rstd[:], 8, norm_c_nr(t, c), links + 1)
                if c == 0:
                    slot_free(t, s)
                dve.tensor_tensor(rows[s][:, c * BANK:(c + 1) * BANK].rearrange("p (h w) -> p h w", w=HD),
                                  ps[c][:].rearrange("p (h w) -> p h w", w=HD),
                                  rstd[:].rearrange("p (h w) -> p h w", w=1).broadcast_to([P, 8, HD]),
                                  ALU.mult).then_inc(out_done[c], 1)

            def silu(t, s, c, n):
                lo = 4 * HD if c == 1 else 0
                w = slice(lo, width[c])
                at = {3: DA, 1: 0, 2: 4 * HD}[c]
                dve.wait_ge(expo_done, t * 3 + n + 1)
                dve.tensor_scalar(denom[:, w], expo[:, w], 1.0, None, ALU.add).then_inc(chain, 1)
                dve.wait_ge(chain, t * 6 + 2 * n + 1)
                dve.reciprocal(denom[:, w], denom[:, w]).then_inc(chain, 1)
                dve.wait_ge(chain, t * 6 + 2 * n + 2)
                if n == 0:
                    slot_free(t, s)
                if c == 1:
                    dve.wait_ge(v_tail_done, t + 1)
                dve.tensor_tensor(gate[s][:, at:at + width[c] - lo], ps[c][:, w], denom[:, w],
                                  ALU.mult).then_inc(out_done[c], 1)

            def step(t, s):
                links = t * TILE_LINKS + 2 * X_LINKS - (X_LINKS if last(t) else 0)
                if half == 0:
                    dve.wait_ge(mm_done[3], t + 1)
                    dve.tensor_copy(u[:], ps[3][:, 0:DF]).then_inc(u_done, 1)
                if not last(t):
                    split(t + 1, 1 - s)
                if half == 0:
                    for c in range(3):
                        if c == 2 and not late(t):
                            norm_x(t + 2, s, links + 2 * C_LINKS)
                            links = links + X_LINKS
                        head_norm(t, s, c, links + c * C_LINKS)
                        if c == 0:
                            dve.wait_ge(ut_done, t + 1)
                            dve.tensor_copy(ut[:], ps[3][:, DF:2 * DF]).then_inc(ut_copied, 1)
                        if c == 1:
                            dve.wait_ge(ab_done, t + 1)
                            dve.tensor_copy(ab[s][:], ps[3][:]).then_inc(out_done[3], 1)
                else:
                    for n, c in enumerate((3, 1, 2)):
                        if n == 2 and not late(t):
                            norm_x(t + 2, s, None)
                        silu(t, s, c, n)

            def split_w(n):
                c, ks = units[n]
                cols = slice(c * BANK, c * BANK + width[c])
                dve.wait_ge(w_hi_done, n + 1)
                dve.tensor_tensor(w_lo[:, ks, cols], stage[n % 2][:, :, 0:width[c]], w_hi[:, ks, cols].bitcast(F32),
                                  ALU.subtract).then_inc(w_lo_done, 1)

            norm_x(0, 0, 0)
            split(0, 0)
            for n in range(len(units)):
                split_w(n)
            norm_x(1, 1, X_LINKS)
            tiles(dve, step)



def fourier(core, name, seq, base):
    nc, io, dram = core.nc, core.io, core.dram
    S = lambda n: core.sem(f"four_{name}_{n}")
    n1 = seq // N2
    rows, quarter, pieces = 2 * n1, N2 * DF // 4, 4
    per_piece = quarter // BANK
    table_in, z_in, first_done, first_out = S("table_in"), [S(f"z_in{i}") for i in range(4)], S("first_done"), S("first_out")
    g_out, g_in = S("g_out"), [S(f"g_in{i}") for i in range(4)]
    second_done, second_out, stored = S("second_done"), S("second_out"), S("stored")
    with ExitStack() as st:
        sb = lambda n, shape: core.sb(st, f"four_{name}_{n}", shape)
        first, second = sb("first", [rows, rows]), sb("second", [2 * N2, n1 * N2])
        z, g = sb("z", [rows, N2 * DF]), sb("g", [rows, N2 * DF])
        g2 = sb("g2", [2 * N2, n1 * DF // 2])
        y = z[0:N2, 0:n1 * DF]
        ps = [core.ps(st, f"four_{name}_ps{i}") for i in range(8)]
        block = st.enter_context(nc.Block())
        tokens = dram["ab"][base:base + seq, :].rearrange("(a b) (s c) -> s a b c", b=N2, s=2)
        g_rows = dram["g_" + name].rearrange("(s k) (n c) -> s n k c", s=2, c=DF)
        out = dram["four"][base:base + seq, :].rearrange("(b a) c -> b a c", a=n1)
        groups = N2 * DF // BANK
        pairs = n1 // 2
        half_k = n1 // 2

        @block.sync
        def _(sp):
            sp.dma_start(first[:], io["c_first_" + name]).then_inc(table_in, 16)
            for i in range(pieces):
                for part in range(2):
                    sp.dma_start(z[part * n1:(part + 1) * n1, i * quarter:(i + 1) * quarter],
                                 tokens[part, :, i * N2 // 4:(i + 1) * N2 // 4, :]).then_inc(z_in[i], 16)
            sp.dma_start(second[:], io["c_second_" + name]).then_inc(table_in, 16)
            for i in range(pieces):
                sp.wait_ge(first_out, per_piece * (i + 1))
                sp.dma_start(dram["g_" + name][:, i * quarter:(i + 1) * quarter],
                             g[:, i * quarter:(i + 1) * quarter]).then_inc(g_out, 16)
            sp.wait_ge(g_out, 16 * pieces)
            for b in range(2):
                if b == 1:
                    sp.wait_ge(second_done, half_k // 2)
                for part in range(2):
                    sp.dma_start(g2[part * N2:(part + 1) * N2, :].rearrange("p (k c) -> p k c", c=DF),
                                 g_rows[part, :, b * half_k:(b + 1) * half_k, :]).then_inc(g_in[b], 16)
                sp.wait_ge(second_out, (b + 1) * half_k // 2)
                sp.dma_start(out[:, b * half_k:(b + 1) * half_k, :],
                             y.rearrange("p (k c) -> p k c", c=DF)[:, b * half_k:(b + 1) * half_k, :]).then_inc(stored, 16)
            sp.wait_ge(stored, 32)

        @block.tensor
        def _(pe):
            pe.wait_ge(table_in, 32)
            for i in range(groups):
                if i % per_piece == 0:
                    pe.wait_ge(z_in[i // per_piece], 32)
                if i >= 8:
                    pe.wait_ge(first_out, i - 7)
                pe.matmul(ps[i % 8][0:rows, :], first[:], z[:, i * BANK:(i + 1) * BANK],
                          start=True, stop=True).then_inc(first_done, 1)
            pe.wait_ge(first_out, groups)
            for i in range(pairs):
                if i % (half_k // 2) == 0:
                    pe.wait_ge(g_in[i // (half_k // 2)], 32)
                if i >= 8:
                    pe.wait_ge(second_out, i - 7)
                for j in range(2):
                    k1 = 2 * i + j
                    kk = k1 % half_k
                    ins = pe.matmul(ps[i % 8][0:N2, j * DF:(j + 1) * DF], second[:, k1 * N2:(k1 + 1) * N2],
                                    g2[:, kk * DF:(kk + 1) * DF], start=True, stop=True)
                ins.then_inc(second_done, 1)

        @block.vector
        def _(dve):
            for i in range(groups):
                dve.wait_ge(first_done, i + 1)
                dve.tensor_copy(g[:, i * BANK:(i + 1) * BANK], ps[i % 8][0:rows, :]).then_inc(first_out, 1)
            for i in range(pairs):
                dve.wait_ge(second_done, i + 1)
                dve.tensor_copy(y[:, i * BANK:(i + 1) * BANK], ps[i % 8][0:N2, :]).then_inc(second_out, 1)



class Group:

    def __init__(self, dil, n, start, lo, hi):
        self.dil, self.n, self.start, self.lo, self.w = dil, n, start, lo, hi - lo
        self.chunks = [min(P, self.w - at) for at in range(0, self.w, P)]
        self.loads = 1 + 2 * len(self.chunks)


def tile_groups():
    a, b = SEQS
    inner, head, tail, alone = (0, 256), (64, 256), (0, 192), (64, 192)
    lane = lambda i, d: i % d
    step = lambda i, d: i // d
    return [
        Group(1, 2, lambda i: i * a, *head),
        Group(1, 2, lambda i: i * b + (a - P), *tail),
        Group(1, a // P - 2, lambda i: i * P + P, *inner),
        Group(1, b // P - 2, lambda i: i * P + (a + P), *inner),
        Group(4, 4 * (a // P // 4 - 2), lambda i: step(i, 4) * (4 * P) + lane(i, 4) + 4 * P, *inner),
        Group(4, 4 * (b // P // 4 - 2), lambda i: step(i, 4) * (4 * P) + lane(i, 4) + (a + 4 * P), *inner),
        Group(4, 8, lambda i: step(i, 4) * a + lane(i, 4), *head),
        Group(4, 8, lambda i: step(i, 4) * b + lane(i, 4) + (a - 4 * P), *tail),
        Group(16, 16, lambda i: i, *head),
        Group(16, 16, lambda i: i + a // 2, *tail),
        Group(16, 16, lambda i: i + a, *alone),
    ]


def attention(core):
    nc, io, dram = core.nc, core.io, core.dram
    S = lambda n: core.sem("att_" + n)
    table_in, gain_done = S("table_in"), S("gain_done")
    rows_in, stored = [S("rows_in0"), S("rows_in1")], [S("stored0"), S("stored1")]
    waited = S("waited")
    turned, qk_copied, scored, biased = S("turned"), S("qk_copied"), S("scored"), S("biased")
    exp_done, p_turned, p_copied, pv_done, o_copied = (S(n) for n in
                                                       ("exp_done", "p_turned", "p_copied", "pv_done", "o_copied"))
    with ExitStack() as st:
        sb = lambda n, shape: core.sb(st, "att_" + n, shape)
        bias = sb("bias", [P, len(DILS), NH, 2 * P])
        gain_q, gain_k = sb("gain_q", [P, 1]), sb("gain_k", [P, 1])
        gain = sb("gain", [P, 2, P])
        q = [sb(f"q{i}", [P, DA]) for i in range(2)]
        k = [sb(f"k{i}", [P, 2, DA]) for i in range(2)]
        v = [sb(f"v{i}", [P, 2, VROW]) for i in range(2)]
        o = [sb(f"o{i}", [P, OROW]) for i in range(2)]
        q_t = [sb(f"q_t{i}", [P, 2, P]) for i in range(2)]
        k_t = [sb(f"k_t{i}", [P, 2 * P]) for i in range(2)]
        s_b = [sb(f"s_b{i}", [P, 2, 2 * P]) for i in range(2)]
        p = [sb(f"p{i}", [P, 2, 2 * P]) for i in range(2)]
        p_t = [sb(f"p_t{i}", [P, 2, 2, P]) for i in range(2)]
        ps_t, ps_p = core.ps(st, "att_ps_t"), core.ps(st, "att_ps_p")
        ps_s = [[core.ps(st, f"att_ps_s{i}{j}") for j in range(2)] for i in range(2)]
        ps_o = [core.ps(st, f"att_ps_o{i}") for i in range(2)]
        block = st.enter_context(nc.Block())
        groups = tile_groups()
        n_tables = len(DILS) + 4

        def runs(engine, prologue, tile):
            done, loads = 0, [0, 0]
            for grp in groups:
                half = grp.n // 2
                prologue(grp, done, loads)
                if half > 1:
                    with engine.Fori(0, half - 1) as it:
                        for s in range(2):
                            tile(grp, done, it * 2 + s, s, tuple(loads), True, s == 0)
                for s in range(2):
                    tile(grp, done, grp.n - 2 + s, s, tuple(loads), False, s == 0)
                done += grp.n
                for s in range(2):
                    loads[s] += 16 * grp.loads * half

        def wait(engine, semaphore, count):
            if not isinstance(count, int) or count > 0:
                engine.wait_ge(semaphore, count)

        @block.sync
        def _(sp):
            sp.dma_start(gain_q[0:HD, :], io["q_norm_g"].rearrange("(p a) -> p a", a=1)).then_inc(table_in, 16)
            sp.dma_start(gain_q[HD:P, :], io["q_norm_g"].rearrange("(p a) -> p a", a=1)).then_inc(table_in, 16)
            sp.dma_start(gain_k[0:HD, :], io["k_norm_g"].rearrange("(p a) -> p a", a=1)).then_inc(table_in, 16)
            sp.dma_start(gain_k[HD:P, :], io["k_norm_g"].rearrange("(p a) -> p a", a=1)).then_inc(table_in, 16)
            for i in range(len(DILS)):
                src = bass.AP(dram["line"].tensor, i * NH * P * LINE + LINE // 2 - 1 - REACH,
                              [[LINE - 1, P], [P * LINE, NH], [1, 2 * P]])
                sp.dma_start(bias[:, i, :, :], src).then_inc(table_in, 16)

            def load(grp, done, i, s):
                at = grp.start(i)
                wait(sp, pv_done, i * PAIRS + PAIRS * (done - 1))
                sp.dma_start(q[s][:], dram["q"][bass.ds(at, P, grp.dil), :]).then_inc(rows_in[s], 16)
                for j, n in enumerate(grp.chunks):
                    key = at + (grp.lo - REACH + j * P) * grp.dil
                    sp.dma_start(k[s][0:n, j, :], dram["k"][bass.ds(key, n, grp.dil), :]).then_inc(rows_in[s], 16)
                    sp.dma_start(v[s][0:n, j, :], dram["v"][bass.ds(key, n, grp.dil), :]).then_inc(rows_in[s], 16)

            def prologue(grp, done, loads):
                load(grp, done, 0, 0)
                load(grp, done, 1, 1)

            def tile(grp, done, i, s, loads, more, even):
                at = grp.start(i)
                if more:
                    load(grp, done, i + 2, s)
                wait(sp, o_copied, i * 2 + 2 * (done + 1))
                wait(sp, biased, i * NH + NH * (done + 1))
                sp.dma_start(dram["o"][DILS.index(grp.dil), bass.ds(at, P, grp.dil), :], o[s][:]).then_inc(stored[s], 16)

            runs(sp, prologue, tile)
            for s in range(2):
                sp.wait_ge(stored[s], 16 * len(DILS) * TILES // 2)

        @block.gpsimd
        def _(pool):
            pool.memset(gain[:], 0.0).then_inc(gain_done, 1)
            pool.wait_ge(gain_done, 1)
            for e in range(2):
                pool.memset(gain[HD * e:HD * (e + 1), e, :], 1.0 / math.sqrt(HD)).then_inc(gain_done, 1)

        @block.tensor
        def _(pe):
            def turn(grp, i, s, g, p_, loads):
                if p_ == 0:
                    pe.wait_ge(rows_in[s], (i - s) * (8 * grp.loads) + (16 * grp.loads + loads[s]))
                wait(pe, qk_copied, g)
                cols = slice(p_ * P, (p_ + 1) * P)
                at = 0
                for j, n in enumerate(grp.chunks):
                    pe.transpose(ps_t[:, at:at + n], k[s][0:n, j, cols], core.ident[0:n, 0:n])
                    at += n
                pe.transpose(ps_t[:, 2 * P:3 * P], q[s][:, cols], core.ident[:]).then_inc(turned, 1)

            def score(grp, g, p_):
                pe.wait_ge(qk_copied, g + 1)
                for e in range(2):
                    wait(pe, biased, g * 2 + (e - 3))
                    pe.matmul(ps_s[p_ % 2][e][:, 0:grp.w], q_t[p_ % 2][:, e, :], k_t[p_ % 2][:, 0:grp.w],
                              start=True, stop=True).then_inc(scored, 1)

            def turn_p(grp, g, p_):
                wait(pe, p_copied, g)
                for e in range(2):
                    pe.wait_ge(exp_done, g * 2 + (e + 1))
                    for j, n in enumerate(grp.chunks):
                        ins = pe.transpose(ps_p[0:n, (2 * e + j) * P:(2 * e + j + 1) * P],
                                           p[p_ % 2][:, e, j * P:j * P + n], core.ident[:])
                ins.then_inc(p_turned, 1)

            def weigh(grp, s, g, p_, tile_nr):
                pe.wait_ge(p_copied, g + 1)
                b = p_ // 3
                if p_ % 3 == 0:
                    wait(pe, o_copied, tile_nr * 2 + (b - 1))
                for e in range(2):
                    at = (2 * p_ + e) * VW
                    to = at - b * 6 * VW
                    for j, n in enumerate(grp.chunks):
                        ins = pe.matmul(ps_o[b][:, to:to + 2 * VW], p_t[p_ % 2][0:n, e, j, :],
                                        v[s][0:n, j, at:at + 2 * VW], start=(j == 0), stop=(j == len(grp.chunks) - 1))
                ins.then_inc(pv_done, 1)

            def prologue(grp, done, loads):
                g = done * PAIRS
                turn(grp, 0, 0, g, 0, loads)
                turn(grp, 0, 0, g + 1, 1, loads)
                score(grp, g, 0)

            def tile(grp, done, i, s, loads, more, even):
                for p_ in range(PAIRS):
                    g = i * PAIRS + (done * PAIRS + p_)
                    turn_p(grp, g, p_)
                    if more or even or p_ + 1 < PAIRS:
                        score(grp, g + 1, (p_ + 1) % PAIRS)
                    if p_ + 2 < PAIRS:
                        turn(grp, i, s, g + 2, p_ + 2, loads)
                    elif more or even:
                        turn(grp, i + 1, 1 - s, g + 2, p_ + 2 - PAIRS, loads)
                    weigh(grp, s, g, p_, i + done)

            runs(pe, prologue, tile)

        @block.scalar
        def _(act):
            def exponent(grp, i, s, g, p_):
                for e in range(2):
                    head = NH * VW + 2 * p_ + e
                    act.wait_ge(biased, g * 2 + (e + 1))
                    if e == 0:
                        wait(act, p_turned, g - 1)
                    act.activation(p[p_ % 2][:, e, 0:grp.w], s_b[p_ % 2][:, e, 0:grp.w], ACT.Exp,
                                   bias=o[s][:, head:head + 1], scale=-1.0).then_inc(exp_done, 1)

            def copy_p(grp, g, p_):
                act.wait_ge(p_turned, g + 1)
                wait(act, pv_done, g - 1)
                src = ps_p[:].rearrange("p (e j q) -> p e j q", e=2, j=2)
                if len(grp.chunks) == 2 and grp.chunks[1] == P:
                    act.activation(p_t[p_ % 2][:], src, ACT.Copy).then_inc(p_copied, 1)
                else:
                    for j, n in enumerate(grp.chunks):
                        ins = act.activation(p_t[p_ % 2][0:n, :, j, :], src[0:n, :, j, :], ACT.Copy)
                    ins.then_inc(p_copied, 1)

            def tile(grp, done, i, s, loads, more, even):
                for p_ in range(PAIRS):
                    g = i * PAIRS + (done * PAIRS + p_)
                    copy_p(grp, g, p_)
                    if p_ + 1 < PAIRS:
                        exponent(grp, i, s, g + 1, p_ + 1)
                    elif more or even:
                        exponent(grp, i + 1, 1 - s, g + 1, 0)

            runs(act, lambda grp, done, loads: exponent(grp, 0, 0, done * PAIRS, 0), tile)

        @block.vector
        def _(dve):
            dve.wait_ge(table_in, 16 * n_tables)
            dve.wait_ge(gain_done, 3)
            dve.tensor_scalar(gain[:], gain[:], gain_q[:], gain_k[:], ALU.mult, ALU.mult).then_inc(gain_done, 1)
            dve.wait_ge(gain_done, 4)

            def copy_qk(grp, g, p_):
                dve.wait_ge(turned, g + 1)
                wait(dve, scored, g * 2 - 2)
                dve.tensor_copy(k_t[p_ % 2][:, 0:grp.w], ps_t[:, 0:grp.w])
                dve.tensor_tensor(q_t[p_ % 2][:], ps_t[:, 2 * P:3 * P].rearrange("p (e c) -> p e c", e=1)
                                  .broadcast_to([P, 2, P]), gain[:], ALU.mult).then_inc(qk_copied, 1)

            def add_bias(grp, i, s, g, p_, tile_nr):
                if p_ == 0 and not (isinstance(tile_nr, int) and tile_nr < 2):
                    dve.wait_ge(stored[s], (tile_nr - s) * 8)
                for e in range(2):
                    head = 2 * p_ + e
                    dve.wait_ge(scored, g * 2 + (e + 1))
                    wait(dve, exp_done, g * 2 + (e - 3))
                    dve.sem_inc(waited, 1)
                    dve.tensor_tensor_reduce(s_b[p_ % 2][:, e, 0:grp.w], ps_s[p_ % 2][e][:, 0:grp.w],
                                             bias[:, DILS.index(grp.dil), head, grp.lo:grp.lo + grp.w], -1.0, -3 * NEG,
                                             ALU.add, ALU.min, o[s][:, NH * VW + head:NH * VW + head + 1]).then_inc(biased, 1)

            def copy_o(s, b, pairs):
                dve.wait_ge(pv_done, pairs)
                dve.tensor_copy(o[s][:, b * 6 * VW:(b + 1) * 6 * VW], ps_o[b][:, 0:6 * VW]).then_inc(o_copied, 1)

            def prologue(grp, done, loads):
                copy_qk(grp, done * PAIRS, 0)
                copy_qk(grp, done * PAIRS + 1, 1)
                add_bias(grp, 0, 0, done * PAIRS, 0, done)

            def tile(grp, done, i, s, loads, more, even):
                for p_ in range(PAIRS):
                    g = i * PAIRS + (done * PAIRS + p_)
                    if p_ + 1 < PAIRS:
                        add_bias(grp, i, s, g + 1, p_ + 1, i + done)
                    elif more or even:
                        add_bias(grp, i + 1, 1 - s, g + 1, 0, i + (done + 1))
                    if p_ + 2 < PAIRS:
                        copy_qk(grp, g + 2, p_ + 2)
                    elif more or even:
                        copy_qk(grp, g + 2, p_ + 2 - PAIRS)
                    if p_ % 3 == 2:
                        copy_o(s, p_ // 3, g + 1)

            runs(dve, prologue, tile)



def combine(core):
    nc, io, dram = core.nc, core.io, core.dram
    S = lambda n: core.sem("out_" + n)
    w_in, w_hi_done, w_lo_done = [S("w_in0"), S("w_in1")], S("w_hi_done"), S("w_lo_done")
    rows_in, x_in, mix_done = [S("rows_in0"), S("rows_in1")], [S("x_in0"), S("x_in1")], S("mix_done")
    shift_done, exp_done, share_done, acc_done = S("shift_done"), S("exp_done"), S("share_done"), S("acc_done")
    t_done, hi_done, lo_done = S("t_done"), S("hi_done"), S("lo_done")
    mm_done, y_done, chain, stored = S("mm_done"), S("y_done"), S("chain"), [S("stored0"), S("stored1")]
    n_d = len(DILS)
    LOADS = n_d + 2
    LINKS = 11
    first = lambda t: isinstance(t, int) and t == 0
    early = lambda t: isinstance(t, int) and t < 2
    late = lambda t: isinstance(t, int) and t >= TILES - 2
    last = lambda t: isinstance(t, int) and t == TILES - 1

    def tiles(engine, step):
        step(0, 0)
        step(1, 1)
        with engine.Fori(1, TILES // 2 - 2) as it:
            step(it * 2, 0)
            step(it * 2 + 1, 1)
        for t in range(TILES - 4, TILES):
            step(t, t % 2)

    with ExitStack() as st:
        sb = lambda n, shape, dt=F32: core.sb(st, "out_" + n, shape, dt)
        w_hi, w_lo = sb("w_hi", [P, KC, D], F32R), sb("w_lo", [P, KC, D], F32R)
        stage = [sb(f"stage{i}", [P, D]) for i in range(2)]
        o = [sb(f"o{i}", [P, n_d, OROW]) for i in range(2)]
        gate = [sb(f"gate{i}", [P, D]) for i in range(2)]
        four = [sb(f"four{i}", [P, DF]) for i in range(2)]
        x = [sb(f"x{i}", [P, D]) for i in range(2)]
        least, shift, weight, part = (sb(n, [P, n_d, NH]) for n in ("least", "shift", "weight", "part"))
        total, inv = sb("total", [P, NH]), sb("inv", [P, NH])
        acc, term = sb("acc", [P, DA]), [sb(f"term{i}", [P, DA]) for i in range(2)]
        mix = [sb(f"mix{i}", [P, D]) for i in range(2)]
        m_hi = [sb(f"m_hi{i}", [P, KC, P], F32R) for i in range(2)]
        m_lo = [sb(f"m_lo{i}", [P, KC, P], F32R) for i in range(2)]
        y = [sb(f"y{i}", [P, D]) for i in range(2)]
        ps_t = [core.ps(st, f"out_ps_t{i}") for i in range(4)]
        ps_y = [core.ps(st, f"out_ps_y{i}") for i in range(4)]
        block = st.enter_context(nc.Block())

        @block.sync
        def _(sp):
            def load_rows(t, s):
                if not early(t):
                    sp.wait_ge(mix_done, t - 1)
                at = bass.ds(t * P, P)
                for i in range(n_d):
                    sp.dma_start(o[s][:, i, :], dram["o"][i, at, :]).then_inc(rows_in[s], 16)
                sp.dma_start(gate[s][:], dram["gate"][at, :]).then_inc(rows_in[s], 16)
                sp.dma_start(four[s][:], dram["four"][at, :]).then_inc(rows_in[s], 16)

            def load_x(t, s):
                sp.dma_start(x[s][:], io["x"][bass.ds(t * P, P), :]).then_inc(x_in[s], 16)

            load_rows(0, 0)
            for k in range(KC):
                if k >= 2:
                    sp.wait_ge(w_lo_done, k - 1)
                sp.dma_start(stage[k % 2][:], io["w_out"][k * P:(k + 1) * P, :]).then_inc(w_in[k % 2], 16)
            load_rows(1, 1)
            load_x(0, 0)
            load_x(1, 1)
            load_rows(2, 0)

            def step(t, s):
                if not (isinstance(t, int) and t + 3 >= TILES):
                    load_rows(t + 3, 1 - s)
                sp.wait_ge(y_done, t * 2 + 2)
                sp.dma_start(io["y"][bass.ds(t * P, P), :], y[s][:]).then_inc(stored[s], 16)
                if not late(t):
                    load_x(t + 2, s)

            tiles(sp, step)
            for s in range(2):
                sp.wait_ge(stored[s], 16 * TILES // 2)

        @block.tensor
        def _(pe):
            def turn(t, s):
                pe.wait_ge(mix_done, t + 1)
                if not early(t):
                    pe.wait_ge(lo_done, t * 2 - 2)
                for j in range(2):
                    for k in range(4):
                        ins = pe.transpose(ps_t[2 * s + j][:, k * P:(k + 1) * P],
                                           mix[s][:, (4 * j + k) * P:(4 * j + k + 1) * P], core.ident[:])
                    ins.then_inc(t_done, 1)

            def step(t, s):
                pe.wait_ge(lo_done, t * 2 + 2)
                for c in range(2):
                    if not early(t):
                        pe.wait_ge(y_done, t * 2 + (c - 3))
                    for k in range(KC):
                        for n, (a, b) in enumerate(((m_hi, w_hi), (m_hi, w_lo), (m_lo, w_hi))):
                            ins = pe.matmul(ps_y[2 * s + c][:], a[s][:, k, :], b[:, k, c * BANK:(c + 1) * BANK],
                                            start=(k == 0 and n == 0), stop=(k == KC - 1 and n == 2))
                    ins.then_inc(mm_done, 1)
                    if c == 0 and not last(t):
                        turn(t + 1, 1 - s)

            turn(0, 0)
            pe.wait_ge(w_lo_done, KC)
            tiles(pe, step)

        @block.scalar
        def _(act):
            def weights(t):
                act.wait_ge(shift_done, t + 1)
                act.activation(weight[:], shift[:], ACT.Exp).then_inc(exp_done, 1)

            def first_term(t, s):
                act.wait_ge(share_done, t + 1)
                for h in range(NH):
                    ins = act.activation(acc[:, h * HD:(h + 1) * HD], o[s][:, 0, h * VW:h * VW + HD], ACT.Copy,
                                         scale=part[:, 0, h:h + 1])
                ins.then_inc(acc_done, 1)

            def split(t, s):
                for j in range(2):
                    act.wait_ge(t_done, t * 2 + j + 1)
                    if j == 0 and not early(t):
                        act.wait_ge(mm_done, t * 2 - 2)
                    ins = act.activation(m_hi[s][:, 4 * j:4 * j + 4, :],
                                         ps_t[2 * s + j][:].rearrange("p (k c) -> p k c", k=4), ACT.Copy)
                    ins.then_inc(hi_done, 1)

            def step(t, s):
                if not late(t):
                    weights(t + 2)
                    first_term(t + 2, s)
                if not last(t):
                    split(t + 1, 1 - s)

            for k in range(KC):
                act.wait_ge(w_in[k % 2], 16 * (k // 2 + 1))
                act.activation(w_hi[:, k, :], stage[k % 2][:], ACT.Copy).then_inc(w_hi_done, 1)
            weights(0)
            first_term(0, 0)
            split(0, 0)
            weights(1)
            first_term(1, 1)
            tiles(act, step)

        @block.vector
        def _(dve):
            for k in range(KC):
                dve.wait_ge(w_hi_done, k + 1)
                dve.tensor_tensor(w_lo[:, k, :], stage[k % 2][:], w_hi[:, k, :].bitcast(F32),
                                  ALU.subtract).then_inc(w_lo_done, 1)

            def mixed(t, s):
                links = t * LINKS
                at = [0]

                def link(ins):
                    at[0] += 1
                    ins.then_inc(chain, 1)
                    dve.wait_ge(chain, links + at[0])

                dve.wait_ge(rows_in[s], (t - s) * (8 * LOADS) + 16 * LOADS)
                low = o[s][:, :, NH * VW:]
                heads = o[s][:, :, 0:NH * VW].rearrange("p i (h w) -> p i h w", w=VW)
                link(dve.tensor_tensor(least[:, 0, :], low[:, 0, :], low[:, 1, :], ALU.min))
                link(dve.tensor_tensor(least[:, 0, :], least[:, 0, :], low[:, 2, :], ALU.min))
                dve.tensor_tensor(shift[:], least[:, 0:1, :].broadcast_to([P, n_d, NH]), low,
                                  ALU.subtract).then_inc(shift_done, 1)
                dve.wait_ge(exp_done, t + 1)
                link(dve.tensor_tensor(part[:], weight[:], heads[:, :, :, HD], ALU.mult))
                link(dve.tensor_tensor(total[:], part[:, 0, :], part[:, 1, :], ALU.add))
                link(dve.tensor_tensor(total[:], total[:], part[:, 2, :], ALU.add))
                link(dve.reciprocal(inv[:], total[:]))
                dve.tensor_tensor(part[:], weight[:], inv[:].rearrange("p (a h) -> p a h", a=1).broadcast_to([P, n_d, NH]),
                                  ALU.mult).then_inc(share_done, 1)
                dve.wait_ge(share_done, t + 1)
                spread = lambda i: part[:, i, :].rearrange("p (h w) -> p h w", w=1).broadcast_to([P, NH, HD])
                term_h = [b[:].rearrange("p (h w) -> p h w", w=HD) for b in term]
                if not early(t):
                    dve.wait_ge(t_done, t * 2 - 2)
                link(dve.tensor_tensor(mix[s][:, DA:], four[s][:], gate[s][:, DA:], ALU.mult))
                for i in range(1, n_d):
                    link(dve.tensor_tensor(term_h[i - 1], heads[:, i, :, 0:HD], spread(i), ALU.mult))
                link(dve.tensor_tensor(term[0][:], term[0][:], term[1][:], ALU.add))
                dve.wait_ge(acc_done, t + 1)
                link(dve.tensor_tensor(term[0][:], term[0][:], acc[:], ALU.add))
                dve.tensor_tensor(mix[s][:, 0:DA], term[0][:], gate[s][:, 0:DA], ALU.mult).then_inc(mix_done, 1)
                assert at[0] == LINKS

            def split(t, s):
                for j in range(2):
                    dve.wait_ge(hi_done, t * 2 + j + 1)
                    dve.tensor_tensor(m_lo[s][:, 4 * j:4 * j + 4, :],
                                      ps_t[2 * s + j][:].rearrange("p (k c) -> p k c", k=4),
                                      m_hi[s][:, 4 * j:4 * j + 4, :].bitcast(F32), ALU.subtract).then_inc(lo_done, 1)

            def add_x(t, s, c):
                dve.wait_ge(mm_done, t * 2 + (c + 1))
                if c == 0:
                    if not early(t):
                        dve.wait_ge(stored[s], (t - s) * 8)
                    dve.wait_ge(x_in[s], (t - s) * 8 + 16)
                cols = slice(c * BANK, (c + 1) * BANK)
                dve.tensor_tensor(y[s][:, cols], ps_y[2 * s + c][:], x[s][:, cols], ALU.add).then_inc(y_done, 1)

            def step(t, s):
                if not late(t):
                    mixed(t + 2, s)
                add_x(t, s, 0)
                if not last(t):
                    split(t + 1, 1 - s)
                add_x(t, s, 1)

            mixed(0, 0)
            split(0, 0)
            mixed(1, 1)
            tiles(dve, step)



def kernel(x_prompt, x_sample, norm_g, w_in, q_norm_g, k_norm_g, rel_bias, w_four, w_out):
    from concourse import bacc
    from concourse.bass_utils import run_bass_kernel_spmd

    nc = bacc.Bacc("TRN2", target_bir_lowering=False, num_devices=1)
    arrays = {"x": np.concatenate([np.asarray(x_prompt)[0], np.asarray(x_sample)[0]], axis=0),
              "norm_g": np.asarray(norm_g)[0], "w_in": np.asarray(w_in)[0], "q_norm_g": np.asarray(q_norm_g)[0],
              "k_norm_g": np.asarray(k_norm_g)[0], "rel_bias": np.asarray(rel_bias),
              "w_four": np.asarray(w_four)[0], "w_out": np.asarray(w_out)[0]}
    arrays.update(constants())
    io = {k: nc.dram_tensor(k, a.shape, mybir.dt.from_np(a.dtype), kind="ExternalInput").ap()
          for k, a in arrays.items()}
    io["y"] = nc.dram_tensor("y", (TOKENS, D), F32, kind="ExternalOutput").ap()
    build(nc, io)
    y = run_bass_kernel_spmd(nc, [arrays], core_ids=[0]).results[0]["y"]
    return y[None, :SEQS[0]], y[None, SEQS[0]:]
```

```python
import math
from contextlib import ExitStack

import numpy as np

import concourse.bass as bass
from concourse import mybir
from concourse.alu_op_type import AluOpType as ALU

F32 = mybir.dt.float32
F32R = mybir.dt.float32r
ACT = mybir.ActivationFunctionType
AX = mybir.AxisListType

P = 128
D = 1024
HD = 64
NH = 12
DA = NH * HD
NG = 4
DF = NG * HD
SEQS = (4096, 2048)
BASES = (0, 4096)
TOKENS = sum(SEQS)
TILES = TOKENS // P
KC = D // P
HALF = 2 * DA + DF
BANK = 512
BUCKETS = 32
MAX_DISTANCE = 1024
EPS = 1e-6
NEG = -1e30
DILS = (1, 4, 16)
TURN, SCORE, EXP, TURN_P = 5, 4, 2, 1
REACH = 64
LINE = 384
VW = HD + 1
VROW = (NH + 1) * VW
OROW = NH * VW + NH
PAIRS = NH // 2
N2 = 64
PIECE = 8 * BANK



def t5_bucket(rel):
    half = BUCKETS // 2
    exact = half // 2
    n = np.abs(rel)
    nf = np.maximum(n, 1).astype(np.float32)
    large = exact + (np.log(nf / np.float32(exact)) / np.float32(math.log(MAX_DISTANCE / exact))
                     * np.float32(half - exact)).astype(np.int32)
    return np.where(rel > 0, half, 0) + np.where(n < exact, n, np.minimum(large, half - 1))


def constants():
    rel = np.arange(LINE) - (LINE // 2 - 1)
    onehot = np.zeros((BUCKETS + 1, len(DILS) * LINE), np.float32)
    for i, dil in enumerate(DILS):
        for j, r in enumerate(rel):
            row = t5_bucket(np.asarray(r * dil)) if abs(r) <= REACH else BUCKETS
            onehot[row, i * LINE + j] = 1.0 if abs(r) <= REACH else NEG
    a = 2 * np.pi * np.outer(np.arange(HD), np.arange(HD)) / HD
    two = np.eye(2)
    chan = np.concatenate([np.kron(two, np.cos(a)), np.kron(two, np.sin(a))], axis=1)
    out = {"c_ident": np.eye(P), "c_onehot": onehot, "c_chan": chan}
    for name, s in zip("ab", SEQS):
        n1 = s // N2
        a = 2 * np.pi * np.outer(np.arange(n1), np.arange(n1)) / n1
        c, sn = np.cos(a), np.sin(a)
        out["c_first_" + name] = np.block([[c, -sn], [-sn, -c]])
        n, k1, k2 = np.arange(N2)[:, None, None], np.arange(n1)[None, :, None], np.arange(N2)[None, None, :]
        a = 2 * np.pi * ((n * (k1 + n1 * k2)) % s) / s
        second = np.concatenate([np.cos(a), np.sin(a)], axis=0) / math.sqrt(s * HD)
        out["c_second_" + name] = second.reshape(2 * N2, n1 * N2)
    return {k: np.ascontiguousarray(v, np.float32) for k, v in out.items()}


class Core:

    def __init__(self, nc, io):
        self.nc, self.io, self.keep = nc, io, ExitStack()

    def sb(self, stack, name, shape, dt=F32):
        return stack.enter_context(self.nc.sbuf_tensor(name, shape, dt))

    def ps(self, stack, name):
        return stack.enter_context(self.nc.psum_tensor(name, [P, BANK], F32))

    def sem(self, name):
        return self.keep.enter_context(self.nc.semaphore(name))


def build(nc, io):
    core = Core(nc, io)
    with core.keep:
        core.ident = core.sb(core.keep, "ident", [P, P])
        core.rstd_x = core.sb(core.keep, "rstd_x", [P, TILES])
        scratch = {"q": [TOKENS, DA], "k": [TOKENS, DA], "v": [TOKENS, VROW], "gate": [TOKENS, D],
                   "ab": [TOKENS, 2 * DF], "four": [TOKENS, DF], "line": [len(DILS), NH, P, LINE],
                   "o": [len(DILS), TOKENS, OROW],
                   "g_a": [2 * SEQS[0] // N2, N2 * DF], "g_b": [2 * SEQS[1] // N2, N2 * DF]}
        core.dram = {k: nc.dram_tensor("scratch_" + k, s, F32, kind="Internal").ap() for k, s in scratch.items()}
        with ExitStack() as tables:
            core.chan_w = core.sb(tables, "chan_w", [P, 2, 2 * P])
            core.line = core.sb(tables, "line", [NH, len(DILS) * LINE])
            setup(core)
            project(core, 0)
        core.four_in = core.sb(core.keep, "four_in0", [P, PIECE])
        core.four_first = {n: core.sb(core.keep, "four_first_" + n, [2 * seq // N2, 2 * seq // N2])
                           for n, seq in zip("ab", SEQS)}
        core.four_in_loaded, core.four_table_in = core.sem("four_loaded0"), core.sem("four_table_in")
        project(core, 1)
        core.q = [core.sb(core.keep, f"att_q{i}", [P, DA]) for i in range(2)]
        core.k = [core.sb(core.keep, f"att_k{i}", [P, 2, DA]) for i in range(2)]
        core.gain_q, core.gain_k = (core.sb(core.keep, "att_" + n, [P, 1]) for n in ("gain_q", "gain_k"))
        core.qk_in, core.gain_in = [core.sem(f"att_qk_in{i}") for i in range(2)], core.sem("att_gain_in")
        fourier(core)
        core.w_out_hi, core.w_out_lo = (core.sb(core.keep, n, [P, KC, D], F32R) for n in ("w_out_hi", "w_out_lo"))
        attention(core)
        combine(core)



def setup(core):
    nc, io, dram = core.nc, core.io, core.dram
    loaded, cleared, mm_done = (core.sem("setup_" + n) for n in ("loaded", "cleared", "mm_done"))
    with ExitStack() as st:
        onehot = core.sb(st, "onehot", [BUCKETS + 1, len(DILS) * LINE])
        rel = core.sb(st, "rel", [BUCKETS + 1, NH])
        line = core.line
        chan = core.sb(st, "chan", [P, 2 * P])
        wf = core.sb(st, "wf", [P, 2, P])
        ps_line = [core.ps(st, f"ps_line{i}") for i in range(len(DILS))]
        ps_chan = [core.ps(st, f"ps_chan{i}") for i in range(2)]
        block = st.enter_context(nc.Block())
        n_loads = 4 + NG

        @block.gpsimd
        def _(pool):
            pool.memset(wf[:], 0.0).then_inc(cleared, 1)
            pool.memset(rel[:], 1.0).then_inc(cleared, 1)

        @block.sync
        def _(sp):
            sp.dma_start(core.ident[:], io["c_ident"]).then_inc(loaded, 16)
            sp.dma_start(onehot[:], io["c_onehot"]).then_inc(loaded, 16)
            sp.dma_start(chan[:], io["c_chan"]).then_inc(loaded, 16)
            sp.wait_ge(cleared, 2)
            sp.dma_start(rel[0:BUCKETS, :], io["rel_bias"]).then_inc(loaded, 16)
            for g in range(NG):
                lo = HD * (g % 2)
                sp.dma_start(wf[lo:lo + HD, g // 2, lo:lo + HD], io["w_four"][g]).then_inc(loaded, 16)

        @block.tensor
        def _(pe):
            pe.wait_ge(loaded, 16 * n_loads)
            for i in range(len(DILS)):
                pe.matmul(ps_line[i][0:NH, 0:LINE], rel[:], onehot[:, i * LINE:(i + 1) * LINE],
                          start=True, stop=True).then_inc(mm_done, 1)
            for gp in range(2):
                for ab in range(2):
                    pe.matmul(ps_chan[gp][:, ab * P:(ab + 1) * P], chan[:, ab * P:(ab + 1) * P], wf[:, gp, :],
                              start=True, stop=True).then_inc(mm_done, 1)

        @block.vector
        def _(dve):
            dve.wait_ge(mm_done, len(DILS) + 2 * 2)
            for i in range(len(DILS)):
                dve.tensor_copy(line[:, i * LINE:(i + 1) * LINE], ps_line[i][0:NH, 0:LINE])
            for gp in range(2):
                dve.tensor_copy(core.chan_w[:, gp, :], ps_chan[gp][:, 0:2 * P])



def project(core, half):
    nc, io, dram = core.nc, core.io, core.dram
    name = lambda n: f"p{half}_{n}"
    S = lambda n: core.sem(name(n))
    STAGES, PARTS = 6, 4
    w_in, w_hi_done, w_lo_done = [S(f"w_in{i}") for i in range(STAGES)], S("w_hi_done"), S("w_lo_done")
    gain_in, x_in, ones_done = S("gain_in"), [S("x_in0"), S("x_in1")], S("ones_done")
    sq_done, root_done, mean_done, h_done = S("sq_done"), S("root_done"), S("mean_done"), S("h_done")
    t_done, hi_done, lo_done = S("t_done"), S("hi_done"), S("lo_done")
    mm_done = [S(f"mm_done{c}") for c in range(4)]
    out_done = [S(f"out_done{c}") for c in range(4)]
    expo_done, chain = S("expo_done"), S("chain")
    v_tail_done, lines_out = S("v_tail_done"), S("lines_out")
    u_done, ut_done, ut_copied, ab_done = S("u_done"), S("ut_done"), S("ut_copied"), S("ab_done")
    stored = [S("stored0"), S("stored1")]
    n_stores = 3 if half == 0 else 2
    order = (3, 0, 1, 2)
    width = [BANK, BANK, BANK, HALF - 3 * BANK]
    source = [half * 2 * DA + c * BANK for c in range(3)] + [4 * DA + half * DF]
    in_part = KC // PARTS
    units = [(c, slice(k, k + in_part)) for c in order for k in range(0, KC, in_part)]

    first = lambda t: isinstance(t, int) and t == 0
    early = lambda t: isinstance(t, int) and t < 2
    late = lambda t: isinstance(t, int) and t >= TILES - 2
    last = lambda t: isinstance(t, int) and t == TILES - 1
    x_loads = lambda t, s: (t - s) * 8 + 16
    slot_stores = lambda t, s: (t - s) * (8 * n_stores)
    norm_x_nr = lambda t: t + 1 if early(t) else t * 4 - 3
    norm_c_nr = lambda t, c: t * 4 + (c + 3 if c < 2 or late(t) else c + 4) - (1 if last(t) else 0)
    X_LINKS, C_LINKS = 5, 6
    TILE_LINKS = X_LINKS + 3 * C_LINKS

    def tiles(engine, step):
        step(0, 0)
        step(1, 1)
        with engine.Fori(1, TILES // 2 - 1) as it:
            step(it * 2, 0)
            step(it * 2 + 1, 1)
        step(TILES - 2, 0)
        step(TILES - 1, 1)

    with ExitStack() as st:
        sb = lambda n, shape, dt=F32: core.sb(st, name(n), shape, dt)
        w_hi, w_lo = sb("w_hi", [P, KC, HALF], F32R), sb("w_lo", [P, KC, HALF], F32R)
        stage = [sb(f"stage{i}", [P, in_part, BANK]) for i in range(STAGES)]
        gain = sb("gain", [P, KC])
        x = [sb(f"x{i}", [P, D]) for i in range(2)]
        h = [sb(f"h{i}", [P, D]) for i in range(2)]
        h_hi = [sb(f"h_hi{i}", [P, KC, P], F32R) for i in range(2)]
        h_lo = [sb(f"h_lo{i}", [P, KC, P], F32R) for i in range(2)]
        if half == 0:
            squares_x, sumsq_x = sb("squares_x", [P, D]), sb("sumsq_x", [P, 1])
            squares = sb("squares", [P, BANK])
            sumsq, mean, root, inv, work, rstd = (sb(n, [P, 8]) for n in
                                                  ("sumsq", "mean", "root", "inv", "work", "rstd"))
            rows = [sb(f"qk{i}", [P, 2 * DA]) for i in range(2)]
            ab = [sb(f"ab{i}", [P, 2 * DF]) for i in range(2)]
            u, ut = sb("u", [P, DF]), sb("ut", [P, 2 * P])
        else:
            rows = [sb(f"v{i}", [P, VROW]) for i in range(2)]
            gate = [sb(f"gate{i}", [P, D]) for i in range(2)]
            expo, denom = sb("expo", [P, BANK]), sb("denom", [P, BANK])
        ps = [core.ps(st, name(f"ps{c}")) for c in range(4)]
        ps_t = [core.ps(st, name(f"ps_t{c}")) for c in range(4)]
        block = st.enter_context(nc.Block())

        @block.gpsimd
        def _(pool):
            if half == 1:
                for i in range(2):
                    pool.memset(rows[i][:], 1.0).then_inc(ones_done, 1)

        @block.sync
        def _(sp):
            def load_x(t, s):
                if not early(t):
                    sp.wait_ge(h_done, t - 1)
                sp.dma_start(x[s][:], io["x"][bass.ds(t * P, P), :]).then_inc(x_in[s], 16)

            load_x(0, 0)
            with nc.allow_non_contiguous_dma(reason="a gain per channel, 4 KiB in all"):
                sp.dma_start(gain[:], io["norm_g"].rearrange("(k p) -> p k", p=P)).then_inc(gain_in, 16)
            w_rows = io["w_in"].rearrange("(k p) n -> p k n", p=P)
            for n, (c, ks) in enumerate(units):
                if n >= STAGES:
                    sp.wait_ge(w_lo_done, n - STAGES + 1)
                sp.dma_start(stage[n % STAGES][:, :, 0:width[c]],
                             w_rows[:, ks, source[c]:source[c] + width[c]]).then_inc(w_in[n % STAGES], 16)
                if n == 0:
                    load_x(1, 1)
            if half == 1:
                for n in "ab":
                    sp.dma_start(core.four_first[n][:], io["c_first_" + n]).then_inc(core.four_table_in, 16)
                load_piece(core, sp, fourier_pieces()[0], core.four_in, core.four_in_loaded)
            else:
                for i in range(len(DILS)):
                    sp.dma_start(dram["line"][i], core.line[:, i * LINE:(i + 1) * LINE]
                                 .rearrange("h (a j) -> h a j", a=1).broadcast_to([NH, P, LINE])).then_inc(lines_out, 16)

            def step(t, s):
                if not late(t):
                    load_x(t + 2, s)
                for c in range(4):
                    sp.wait_ge(out_done[c], t + 1)
                to = bass.ds(t * P, P)
                if half == 0:
                    sp.dma_start(dram["q"][to, :], rows[s][:, 0:DA]).then_inc(stored[s], 16)
                    sp.dma_start(dram["k"][to, :], rows[s][:, DA:2 * DA]).then_inc(stored[s], 16)
                    sp.dma_start(dram["ab"][to, :], ab[s][:]).then_inc(stored[s], 16)
                else:
                    sp.dma_start(dram["v"][to, :], rows[s][:]).then_inc(stored[s], 16)
                    sp.dma_start(dram["gate"][to, :], gate[s][:]).then_inc(stored[s], 16)

            tiles(sp, step)
            for s in range(2):
                sp.wait_ge(stored[s], 16 * n_stores * (TILES // 2))
            if half == 0:
                sp.wait_ge(lines_out, 16 * len(DILS))

        @block.tensor
        def _(pe):
            def turn(t, s):
                pe.wait_ge(h_done, t + 1)
                if not early(t):
                    pe.wait_ge(lo_done, t * 2 - 2)
                for j in range(2):
                    for k in range(4):
                        ins = pe.transpose(ps_t[2 * s + j][:, k * P:(k + 1) * P],
                                           h[s][:, (4 * j + k) * P:(4 * j + k + 1) * P], core.ident[:])
                    ins.then_inc(t_done, 1)

            def product(t, s, c):
                if not first(t):
                    pe.wait_ge(out_done[c], t)
                cols = slice(c * BANK, c * BANK + width[c])
                for k in range(KC):
                    if first(t) and k % in_part == 0:
                        pe.wait_ge(w_lo_done, PARTS * order.index(c) + k // in_part + 1)
                    for n, (a, b) in enumerate(((h_hi, w_hi), (h_hi, w_lo), (h_lo, w_hi))):
                        ins = pe.matmul(ps[c][:, 0:width[c]], a[s][:, k, :], b[:, k, cols],
                                        start=(k == 0 and n == 0), stop=(k == KC - 1 and n == 2))
                ins.then_inc(mm_done[c], 1)

            def turn_u(t):
                pe.wait_ge(u_done, t + 1)
                for j in range(2):
                    ins = pe.transpose(ps[3][:, DF + j * P:DF + (j + 1) * P], u[:, j * P:(j + 1) * P], core.ident[:])
                ins.then_inc(ut_done, 1)

            def channel_dft(t):
                pe.wait_ge(ut_copied, t + 1)
                to = ps[3][:].rearrange("p (ab j c) -> p ab j c", ab=2, j=2)
                for j in range(2):
                    ins = pe.matmul(to[:, :, j, :], ut[:, j * P:(j + 1) * P],
                                    core.chan_w[:, j, :].rearrange("p (ab c) -> p ab c", ab=2),
                                    start=True, stop=True)
                ins.then_inc(ab_done, 1)

            def step(t, s):
                pe.wait_ge(lo_done, t * 2 + 2)
                for n, c in enumerate(order):
                    product(t, s, c)
                    if n == 0 and not last(t):
                        turn(t + 1, 1 - s)
                    if half == 0 and n == (3 if first(t) else 1):
                        turn_u(t)
                    if half == 0 and n == (3 if first(t) else 2):
                        channel_dft(t)

            turn(0, 0)
            tiles(pe, step)

        @block.scalar
        def _(act):
            def norm_x(t, s):
                act.wait_ge(x_in[s], x_loads(t, s))
                act.activation(squares_x[:], x[s][:], ACT.Square, accum_out=sumsq_x[:, 0:1]).then_inc(sq_done, 1)
                act.wait_ge(mean_done, norm_x_nr(t))
                act.activation(root[:, 0:1], mean[:, 0:1], ACT.Sqrt).then_inc(root_done, 1)

            def split(t, s):
                for j in range(2):
                    act.wait_ge(t_done, t * 2 + j + 1)
                    if j == 0 and not early(t):
                        act.wait_ge(mm_done[order[-1]], t - 1)
                    for k in range(4):
                        ins = act.activation(h_hi[s][:, 4 * j + k, :], ps_t[2 * s + j][:, k * P:(k + 1) * P],
                                             ACT.Copy, scale=gain[:, 4 * j + k:4 * j + k + 1])
                    ins.then_inc(hi_done, 1)

            def head_squares(t, c):
                act.wait_ge(mm_done[c], t + 1)
                act.activation(squares[:], ps[c][:], ACT.Square).then_inc(sq_done, 1)
                act.wait_ge(mean_done, norm_c_nr(t, c))
                act.activation(root[:], mean[:], ACT.Sqrt).then_inc(root_done, 1)

            def values(t, s, c):
                if c == 0 and not early(t):
                    act.wait_ge(stored[s], slot_stores(t, s))
                n = 8 if c == 0 else 4
                act.activation(rows[s][:, 0:NH * VW].rearrange("p (h w) -> p h w", w=VW)[:, 8 * c:8 * c + n, 0:HD],
                               ps[c][:, 0:n * HD].rearrange("p (h w) -> p h w", w=HD),
                               ACT.Copy).then_inc(out_done[0] if c == 0 else v_tail_done, 1)

            def gate_exp(t, c):
                lo = 4 * HD if c == 1 else 0
                before = {3: 2, 1: 3, 2: 1}[c]
                if not (first(t) and c == 3):
                    act.wait_ge(out_done[before], t if c == 3 else t + 1)
                act.activation(expo[:, lo:width[c]], ps[c][:, lo:width[c]], ACT.Exp,
                               scale=-1.0).then_inc(expo_done, 1)

            def step(t, s):
                if not last(t):
                    split(t + 1, 1 - s)
                if half == 0:
                    for c in range(3):
                        if c == 2 and not late(t):
                            norm_x(t + 2, s)
                        head_squares(t, c)
                else:
                    for c in order:
                        act.wait_ge(mm_done[c], t + 1)
                        if c < 2:
                            values(t, s, c)
                        if c > 0:
                            gate_exp(t, c)

            def split_w(n):
                c, ks = units[n]
                act.wait_ge(w_in[n % STAGES], 16 * (n // STAGES + 1))
                act.activation(w_hi[:, ks, c * BANK:c * BANK + width[c]], stage[n % STAGES][:, :, 0:width[c]],
                               ACT.Copy).then_inc(w_hi_done, 1)

            act.wait_ge(gain_in, 16)
            if half == 0:
                norm_x(0, 0)
            else:
                act.wait_ge(ones_done, 2)
            split(0, 0)
            for n in range(len(units)):
                if n == PARTS and half == 0:
                    norm_x(1, 1)
                split_w(n)
            tiles(act, step)

        @block.vector
        def _(dve):
            def rsqrt(out, n, roots, links):
                dve.wait_ge(root_done, roots)
                dve.reciprocal(inv[:, 0:n], root[:, 0:n]).then_inc(chain, 1)
                dve.wait_ge(chain, links + 1)
                dve.tensor_tensor(work[:, 0:n], inv[:, 0:n], inv[:, 0:n], ALU.mult).then_inc(chain, 1)
                dve.wait_ge(chain, links + 2)
                dve.tensor_tensor(work[:, 0:n], work[:, 0:n], mean[:, 0:n], ALU.mult).then_inc(chain, 1)
                dve.wait_ge(chain, links + 3)
                dve.tensor_scalar(work[:, 0:n], work[:, 0:n], -0.5, 1.5, ALU.mult, ALU.add).then_inc(chain, 1)
                dve.wait_ge(chain, links + 4)
                dve.tensor_tensor(out, inv[:, 0:n], work[:, 0:n], ALU.mult).then_inc(chain, 1)
                dve.wait_ge(chain, links + 5)

            def norm_x(t, s, links):
                kept = core.rstd_x[:, bass.ds(t, 1)]
                if half == 0:
                    dve.wait_ge(sq_done, norm_x_nr(t))
                    dve.tensor_scalar(mean[:, 0:1], sumsq_x[:, 0:1], 1.0 / D, EPS, ALU.mult,
                                      ALU.add).then_inc(mean_done, 1)
                    rsqrt(kept, 1, norm_x_nr(t), links)
                else:
                    dve.wait_ge(x_in[s], x_loads(t, s))
                if not early(t):
                    dve.wait_ge(t_done, t * 2 - 2)
                dve.tensor_scalar(h[s][:], x[s][:], kept, None, ALU.mult).then_inc(h_done, 1)

            def split(t, s):
                for j in range(2):
                    dve.wait_ge(hi_done, t * 2 + j + 1)
                    for k in range(4):
                        kk = 4 * j + k
                        ins = dve.scalar_tensor_tensor(h_lo[s][:, kk, :], ps_t[2 * s + j][:, k * P:(k + 1) * P],
                                                       gain[:, kk:kk + 1], h_hi[s][:, kk, :].bitcast(F32),
                                                       ALU.mult, ALU.subtract)
                    ins.then_inc(lo_done, 1)

            def slot_free(t, s):
                if not early(t):
                    dve.wait_ge(stored[s], slot_stores(t, s))

            def head_norm(t, s, c, links):
                dve.wait_ge(sq_done, norm_c_nr(t, c))
                dve.tensor_reduce(sumsq[:], squares[:].rearrange("p (h w) -> p h w", w=HD), AX.X,
                                  ALU.add).then_inc(chain, 1)
                dve.wait_ge(chain, links + 1)
                dve.tensor_scalar(mean[:], sumsq[:], 1.0 / HD, EPS, ALU.mult, ALU.add).then_inc(mean_done, 1)
                rsqrt(rstd[:], 8, norm_c_nr(t, c), links + 1)
                if c == 0:
                    slot_free(t, s)
                dve.tensor_tensor(rows[s][:, c * BANK:(c + 1) * BANK].rearrange("p (h w) -> p h w", w=HD),
                                  ps[c][:].rearrange("p (h w) -> p h w", w=HD),
                                  rstd[:].rearrange("p (h w) -> p h w", w=1).broadcast_to([P, 8, HD]),
                                  ALU.mult).then_inc(out_done[c], 1)

            def silu(t, s, c, n):
                lo = 4 * HD if c == 1 else 0
                w = slice(lo, width[c])
                at = {3: DA, 1: 0, 2: 4 * HD}[c]
                dve.wait_ge(expo_done, t * 3 + n + 1)
                dve.tensor_scalar(denom[:, w], expo[:, w], 1.0, None, ALU.add).then_inc(chain, 1)
                dve.wait_ge(chain, t * 6 + 2 * n + 1)
                dve.reciprocal(denom[:, w], denom[:, w]).then_inc(chain, 1)
                dve.wait_ge(chain, t * 6 + 2 * n + 2)
                if n == 0:
                    slot_free(t, s)
                if c == 1:
                    dve.wait_ge(v_tail_done, t + 1)
                dve.tensor_tensor(gate[s][:, at:at + width[c] - lo], ps[c][:, w], denom[:, w],
                                  ALU.mult).then_inc(out_done[c], 1)

            def step(t, s):
                links = t * TILE_LINKS + 2 * X_LINKS - (X_LINKS if last(t) else 0)
                if half == 0:
                    dve.wait_ge(mm_done[3], t + 1)
                    dve.tensor_copy(u[:], ps[3][:, 0:DF]).then_inc(u_done, 1)
                if not last(t):
                    split(t + 1, 1 - s)
                if half == 0:
                    for c in range(3):
                        if c == 2 and not late(t):
                            norm_x(t + 2, s, links + 2 * C_LINKS)
                            links = links + X_LINKS
                        head_norm(t, s, c, links + c * C_LINKS)
                        if c == 0:
                            dve.wait_ge(ut_done, t + 1)
                            dve.tensor_copy(ut[:], ps[3][:, DF:2 * DF]).then_inc(ut_copied, 1)
                        if c == 1:
                            dve.wait_ge(ab_done, t + 1)
                            dve.tensor_copy(ab[s][:], ps[3][:]).then_inc(out_done[3], 1)
                else:
                    for n, c in enumerate((3, 1, 2)):
                        if n == 2 and not late(t):
                            norm_x(t + 2, s, None)
                        silu(t, s, c, n)

            def split_w(n):
                c, ks = units[n]
                cols = slice(c * BANK, c * BANK + width[c])
                dve.wait_ge(w_hi_done, n + 1)
                dve.tensor_tensor(w_lo[:, ks, cols], stage[n % STAGES][:, :, 0:width[c]], w_hi[:, ks, cols].bitcast(F32),
                                  ALU.subtract).then_inc(w_lo_done, 1)

            norm_x(0, 0, 0)
            split(0, 0)
            for n in range(len(units)):
                if n == PARTS:
                    norm_x(1, 1, X_LINKS)
                split_w(n)
            tiles(dve, step)



class Piece:

    def __init__(self, name, seq, base, level, i):
        self.name, self.seq, self.base, self.level, self.i = name, seq, base, level, i
        self.n1 = seq // N2
        self.rows = 2 * self.n1 if level == 1 else 2 * N2
        self.out_rows = 2 * self.n1 if level == 1 else N2


def fourier_pieces():
    both, each = list(zip("ab", SEQS, BASES)), PIECE // DF
    return ([Piece(*seq, 1, i) for seq in both for i in range(N2 // each)]
            + [Piece(*seq, 2, i) for seq in both for i in range(seq[1] // N2 // each)])


def load_piece(core, sp, at, to, loaded):
    each = slice(at.i * PIECE // DF, (at.i + 1) * PIECE // DF)
    if at.level == 1:
        src = core.dram["ab"][at.base:at.base + at.seq, :].rearrange("(a b) (s c) -> s a b c", b=N2, s=2)
    else:
        src = core.dram["g_" + at.name].rearrange("(s k) (n c) -> s n k c", s=2, c=DF)
    half = at.rows // 2
    for part in range(2):
        sp.dma_start(to[part * half:(part + 1) * half, :].rearrange("p (n c) -> p n c", c=DF),
                     src[part, :, each, :]).then_inc(loaded, 16)


def fourier(core):
    nc, io, dram = core.nc, core.io, core.dram
    S = lambda n: core.sem("four_" + n)
    BANKS, IN, OUT = 8, 6, 4
    k1s = PIECE // DF
    pieces = fourier_pieces()
    fine_in = S("fine_in")
    loaded = [core.four_in_loaded] + [S(f"loaded{i}") for i in range(1, IN)]
    mm_done, out_done = S("mm_done"), [S("dve_out"), S("act_out")]
    stored = [S(f"stored{i}") for i in range(OUT)]
    with ExitStack() as st:
        sb = lambda n, shape: core.sb(st, "four_" + n, shape)
        first = core.four_first
        second = {n: sb("second_" + n, [2 * N2, seq]) for n, seq in zip("ab", SEQS)}
        source = [core.four_in] + [sb(f"in{i}", [P, PIECE]) for i in range(1, IN)]
        result = [sb(f"out{i}", [P, PIECE]) for i in range(OUT)]
        ps = [core.ps(st, f"four_ps{i}") for i in range(BANKS)]
        block = st.enter_context(nc.Block())

        @block.sync
        def _(sp):
            def load(m):
                if m >= IN:
                    sp.wait_ge(mm_done, BANKS * (m - IN + 1))
                load_piece(core, sp, pieces[m], source[m % IN], loaded[m % IN])

            def store(m):
                at = pieces[m]
                for evac in out_done:
                    sp.wait_ge(evac, BANKS // 2 * (m + 1))
                have = result[m % OUT][0:at.out_rows, :]
                if at.level == 1:
                    to = dram["g_" + at.name][:, at.i * PIECE:(at.i + 1) * PIECE]
                else:
                    to = dram["four"][at.base:at.base + at.seq, :].rearrange("(b a) c -> b a c", a=at.n1)
                    to = to[:, at.i * k1s:(at.i + 1) * k1s, :]
                    have = have.rearrange("p (k c) -> p k c", c=DF)
                sp.dma_start(to, have).then_inc(stored[m % OUT], 16)

            def spectrum_stored(name):
                for m, at in enumerate(pieces):
                    if at.level == 1 and at.name == name:
                        sp.wait_ge(stored[m % OUT], 16 * (m // OUT + 1))

            for m in range(1, IN):
                load(m)
                if m == 4:
                    for n in "ab":
                        sp.dma_start(second[n][:], io["c_second_" + n]).then_inc(fine_in, 16)
            ready = IN
            for m, at in enumerate(pieces):
                store(m)
                while ready < len(pieces) and ready - IN <= m:
                    new = pieces[ready]
                    if new.level == 2:
                        last_g = max(i for i, x in enumerate(pieces) if x.level == 1 and x.name == new.name)
                        if m < last_g + (1 if new.name == "a" else 0):
                            break
                        if new.i == 0:
                            spectrum_stored(new.name)
                    load(ready)
                    ready += 1
            for to, g in ((core.gain_q, "q_norm_g"), (core.gain_k, "k_norm_g")):
                for e in range(2):
                    sp.dma_start(to[e * HD:(e + 1) * HD, :], io[g].rearrange("(p a) -> p a", a=1)).then_inc(core.gain_in, 16)
            for i in range(2):
                load_qk(core, sp, tile_groups()[0], i, i)
            for i in range(OUT):
                sp.wait_ge(stored[i], 16 * len(range(i, len(pieces), OUT)))

        @block.tensor
        def _(pe):
            pe.wait_ge(core.four_table_in, 32)
            for m, at in enumerate(pieces):
                have = source[m % IN][0:at.rows, :]
                pe.wait_ge(loaded[m % IN], 32 * (m // IN + 1))
                if at.level == 2:
                    pe.wait_ge(fine_in, 32)
                for j in range(BANKS):
                    if m >= 1:
                        pe.wait_ge(out_done[j % 2], BANKS // 2 * (m - 1) + j // 2 + 1)
                    if at.level == 1:
                        ins = pe.matmul(ps[j][0:at.out_rows, :], first[at.name][:], have[:, j * BANK:(j + 1) * BANK],
                                        start=True, stop=True)
                    else:
                        for i in range(2 * j, 2 * j + 2):
                            k1 = at.i * k1s + i
                            ins = pe.matmul(ps[j][0:N2, i % 2 * DF:(i % 2 + 1) * DF],
                                            second[at.name][:, k1 * N2:(k1 + 1) * N2],
                                            have[:, i * DF:(i + 1) * DF], start=True, stop=True)
                    ins.then_inc(mm_done, 1)

        def copies(engine, parity):
            for m, at in enumerate(pieces):
                if m >= OUT:
                    engine.wait_ge(stored[m % OUT], 16 * (m // OUT))
                for j in range(parity, BANKS, 2):
                    engine.wait_ge(mm_done, BANKS * m + j + 1)
                    to, have = result[m % OUT][0:at.out_rows, j * BANK:(j + 1) * BANK], ps[j][0:at.out_rows, :]
                    ins = engine.activation(to, have, ACT.Copy) if parity else engine.tensor_copy(to, have)
                    ins.then_inc(out_done[parity], 1)

        @block.vector
        def _(dve):
            copies(dve, 0)

        @block.scalar
        def _(act):
            copies(act, 1)



class Group:

    def __init__(self, dil, n, start, lo, hi):
        self.dil, self.n, self.start, self.lo, self.w = dil, n, start, lo, hi - lo
        self.chunks = [min(P, self.w - at) for at in range(0, self.w, P)]


class Place:

    def __init__(self, grp, i, s, base, before, following):
        self.grp, self.i, self.s, self.base, self.before, self.following = grp, i, s, base, before, following
        self.nr = i + base

    def pair(self, p_):
        return self.i * PAIRS + (self.base * PAIRS + p_)

    def ahead(self, p_):
        if p_ < PAIRS:
            return self, p_
        if not (isinstance(self.i, int) and self.i == self.grp.n - 1):
            return Place(self.grp, self.i + 1, 1 - self.s, self.base, self.before, self.following), p_ - PAIRS
        return self.following and (self.following, p_ - PAIRS)


def tile_groups():
    a, b = SEQS
    inner, head, tail, alone = (0, 256), (64, 256), (0, 192), (64, 192)
    lane = lambda i, d: i % d
    step = lambda i, d: i // d
    return [
        Group(1, 2, lambda i: i * a, *head),
        Group(1, 2, lambda i: i * b + (a - P), *tail),
        Group(1, a // P - 2, lambda i: i * P + P, *inner),
        Group(1, b // P - 2, lambda i: i * P + (a + P), *inner),
        Group(4, 4 * (a // P // 4 - 2), lambda i: step(i, 4) * (4 * P) + lane(i, 4) + 4 * P, *inner),
        Group(4, 4 * (b // P // 4 - 2), lambda i: step(i, 4) * (4 * P) + lane(i, 4) + (a + 4 * P), *inner),
        Group(4, 8, lambda i: step(i, 4) * a + lane(i, 4), *head),
        Group(4, 8, lambda i: step(i, 4) * b + lane(i, 4) + (a - 4 * P), *tail),
        Group(16, 16, lambda i: i, *head),
        Group(16, 16, lambda i: i + a // 2, *tail),
        Group(16, 16, lambda i: i + a, *alone),
    ]


def load_qk(core, sp, grp, i, s):
    row = grp.start(i)
    sp.dma_start(core.q[s][:], core.dram["q"][bass.ds(row, P, grp.dil), :]).then_inc(core.qk_in[s], 16)
    for j, n in enumerate(grp.chunks):
        key = row + (grp.lo - REACH + j * P) * grp.dil
        sp.dma_start(core.k[s][0:n, j, :], core.dram["k"][bass.ds(key, n, grp.dil), :]).then_inc(core.qk_in[s], 16)


def attention(core):
    nc, io, dram = core.nc, core.io, core.dram
    S = lambda n: core.sem("att_" + n)
    bias_in, gain_done, cleared = [S(f"bias_in{i}") for i in range(3)], S("gain_done"), S("cleared")
    w_in, w_hi_done, w_lo_done = S("w_in"), S("w_hi_done"), S("w_lo_done")
    hi_done = S("hi_done")
    qk_in, table_in = core.qk_in, core.gain_in
    v_in, stored = ([S(f"{n}{i}") for i in range(2)] for n in ("v_in", "stored"))
    waited = S("waited")
    turned, qk_copied, scored, biased = S("turned"), S("qk_copied"), S("scored"), S("biased")
    exp_done, p_turned, p_copied, pv_done, o_copied = (S(n) for n in
                                                       ("exp_done", "p_turned", "p_copied", "pv_done", "o_copied"))
    with ExitStack() as st:
        sb = lambda n, shape, dt=F32: core.sb(st, "att_" + n, shape, dt)
        bias = sb("bias", [P, len(DILS), NH, 2 * P])
        gain_q, gain_k, gain = core.gain_q, core.gain_k, sb("gain", [P, 1])
        zeros = sb("zeros", [P, 2, P])
        q, k = core.q, core.k
        v = [sb(f"v{i}", [P, 2, VROW]) for i in range(2)]
        o = [sb(f"o{i}", [P, OROW]) for i in range(2)]
        rest = sb("stage", [P, KC * D - PIECE])
        stage = [core.four_in[:, n * D:(n + 1) * D] for n in range(PIECE // D)]
        stage += [rest[:, n * D:(n + 1) * D] for n in range(KC - PIECE // D)]
        q_hi = [sb(f"q_hi{i}", [P, 2, P], F32R) for i in range(2)]
        q_lo = [sb(f"q_lo{i}", [P, 2, P], F32R) for i in range(2)]
        k_hi = [sb(f"k_hi{i}", [P, 2 * P], F32R) for i in range(2)]
        k_lo = [sb(f"k_lo{i}", [P, 2 * P], F32R) for i in range(2)]
        q_all = [sb(f"q_all{i}", [P, 2, P]) for i in range(2)]
        k_all = [sb(f"k_all{i}", [P, P]) for i in range(2)]
        s_b = [sb(f"s_b{i}", [P, 2, 2 * P]) for i in range(3)]
        p = [sb(f"p{i}", [P, 2, 2 * P]) for i in range(2)]
        p_t = [sb(f"p_t{i}", [P, 2, 2, P]) for i in range(2)]
        ps_t, ps_p = [core.ps(st, f"att_ps_t{i}") for i in range(2)], core.ps(st, "att_ps_p")
        ps_s = [core.ps(st, f"att_ps_s{i}") for i in range(3)]
        ps_o = [core.ps(st, f"att_ps_o{i}") for i in range(2)]
        block = st.enter_context(nc.Block())
        groups = tile_groups()
        split_at = list(range(1, KC + 1))

        def runs(engine, prologue, tile, between=None):
            done, loads = 0, [0, 0]
            starts = []
            for grp in groups:
                starts.append((done, tuple(loads)))
                done += grp.n
                for s in range(2):
                    loads[s] += 16 * len(grp.chunks) * (grp.n // 2)
            prologue(Place(groups[0], 0, 0, 0, (0, 0), None))
            for n, grp in enumerate(groups):
                if between:
                    between(n)
                base, before = starts[n]
                following = Place(groups[n + 1], 0, 0, *starts[n + 1], None) if n + 1 < len(groups) else None
                half = grp.n // 2
                if half > 1:
                    with engine.Fori(0, half - 1) as it:
                        for s in range(2):
                            tile(Place(grp, it * 2 + s, s, base, before, following), True)
                for s in range(2):
                    tile(Place(grp, grp.n - 2 + s, s, base, before, following), False)

        def wait(engine, semaphore, count):
            if not isinstance(count, int) or count > 0:
                engine.wait_ge(semaphore, count)

        @block.sync
        def _(sp):
            def load_v(at, i, s):
                grp = at.grp
                wait(sp, pv_done, i * PAIRS + PAIRS * (at.base - 1))
                for j, n in enumerate(grp.chunks):
                    key = grp.start(i) + (grp.lo - REACH + j * P) * grp.dil
                    sp.dma_start(v[s][0:n, j, :], dram["v"][bass.ds(key, n, grp.dil), :]).then_inc(v_in[s], 16)

            def load(at, i, s):
                wait(sp, turned, i * PAIRS + PAIRS * (at.base - 1))
                load_qk(core, sp, at.grp, i, s)
                load_v(at, i, s)

            def prologue(at):
                load_v(at, 0, 0)
                load_v(at, 1, 1)
                for i in range(len(DILS)):
                    src = bass.AP(dram["line"].tensor, i * NH * P * LINE + LINE // 2 - 1 - REACH,
                                  [[LINE - 1, P], [P * LINE, NH], [1, 2 * P]])
                    sp.dma_start(bias[:, i, :, :], src).then_inc(bias_in[i], 16)
                for k_ in range(KC):
                    sp.dma_start(stage[k_], io["w_out"][k_ * P:(k_ + 1) * P, :]).then_inc(w_in, 16)

            def tile(at, more):
                if more:
                    load(at, at.i + 2, at.s)
                elif at.following:
                    load(at.following, at.s, at.s)
                wait(sp, o_copied, at.i * 2 + 2 * (at.base + 1))
                wait(sp, biased, at.i * NH + NH * (at.base + 1))
                sp.dma_start(dram["o"][DILS.index(at.grp.dil), bass.ds(at.grp.start(at.i), P, at.grp.dil), :],
                             o[at.s][:]).then_inc(stored[at.s], 16)

            runs(sp, prologue, tile)
            for s in range(2):
                sp.wait_ge(stored[s], 16 * len(DILS) * TILES // 2)

        @block.gpsimd
        def _(pool):
            pool.memset(zeros[:], 0.0).then_inc(cleared, 1)
            for i in range(2):
                pool.memset(q_all[i][:], 0.0).then_inc(cleared, 1)

        @block.tensor
        def _(pe):
            def turn(at, p_):
                grp, s, g = at.grp, at.s, at.pair(p_)
                if p_ == 0:
                    pe.wait_ge(qk_in[s], (at.i - s) * (8 * len(grp.chunks) + 8)
                               + (16 * len(grp.chunks) + 16 + at.before[s] + 8 * at.base))
                wait(pe, qk_copied, g - 1)
                cols = slice(p_ * P, (p_ + 1) * P)
                to = 0
                for j, n in enumerate(grp.chunks):
                    pe.transpose(ps_t[p_ % 2][:, to:to + n], k[s][0:n, j, cols], core.ident[0:n, 0:n])
                    to += n
                pe.transpose(ps_t[p_ % 2][:, 2 * P:3 * P], q[s][:, cols], core.ident[:]).then_inc(turned, 1)

            def score(at, p_):
                w, g, b = at.grp.w, at.pair(p_), p_ % 2
                pe.wait_ge(qk_copied, g + 1)
                for e in range(2):
                    wait(pe, biased, g * 2 + (e - 2))
                    to = ps_s[(2 * p_ + e) % 3][:, 0:w]
                    if w == P:
                        ins = pe.matmul(to, q_all[b][:, e, :], k_all[b][:], start=True, stop=True)
                    else:
                        for n, (x, y) in enumerate(((q_hi, k_hi), (q_hi, k_lo), (q_lo, k_hi))):
                            ins = pe.matmul(to, x[b][:, e, :], y[b][:, 0:w], start=(n == 0), stop=(n == 2))
                    ins.then_inc(scored, 1)

            def turn_p(at, p_):
                g = at.pair(p_)
                wait(pe, p_copied, g)
                for e in range(2):
                    pe.wait_ge(exp_done, g * 2 + (e + 1))
                    for j, n in enumerate(at.grp.chunks):
                        ins = pe.transpose(ps_p[0:n, (2 * e + j) * P:(2 * e + j + 1) * P],
                                           p[p_ % 2][:, e, j * P:j * P + n], core.ident[:])
                ins.then_inc(p_turned, 1)

            def weigh(at, p_):
                chunks = at.grp.chunks
                pe.wait_ge(p_copied, at.pair(p_) + 1)
                b = p_ // 3
                if p_ == 0:
                    pe.wait_ge(v_in[at.s], (at.i - at.s) * (8 * len(chunks)) + (16 * len(chunks) + at.before[at.s]))
                if p_ % 3 == 0:
                    wait(pe, o_copied, at.nr * 2 + (b - 1))
                for e in range(2):
                    col = (2 * p_ + e) * VW
                    to = col - b * 6 * VW
                    for j, n in enumerate(chunks):
                        ins = pe.matmul(ps_o[b][:, to:to + 2 * VW], p_t[p_ % 2][0:n, e, j, :],
                                        v[at.s][0:n, j, col:col + 2 * VW], start=(j == 0), stop=(j == len(chunks) - 1))
                ins.then_inc(pv_done, 1)

            def prologue(at):
                turn(at, 0)
                for p_ in range(1, TURN):
                    turn(at, p_)
                    score(at, p_ - 1)
                turn_p(at, 0)

            def tile(at, more):
                for p_ in range(PAIRS):
                    if at.ahead(p_ + TURN_P):
                        turn_p(*at.ahead(p_ + TURN_P))
                    if at.ahead(p_ + TURN):
                        turn(*at.ahead(p_ + TURN))
                    if at.ahead(p_ + SCORE):
                        score(*at.ahead(p_ + SCORE))
                    weigh(at, p_)

            runs(pe, prologue, tile)

        @block.scalar
        def _(act):
            def upper(at, p_):
                w, g = at.grp.w, at.pair(p_)
                act.wait_ge(turned, g + 1)
                wait(act, scored, g * 2 - 2)
                to = k_all[p_ % 2][:] if w == P else k_hi[p_ % 2][:, 0:w]
                act.activation(to, ps_t[p_ % 2][:, 0:w], ACT.Copy, scale=gain[:])
                for e in range(1 if w == P else 2):
                    rows = slice(HD * e, HD * (e + 1))
                    to = (q_all if w == P else q_hi)[p_ % 2]
                    ins = act.activation(to[rows, e, :], ps_t[p_ % 2][rows, 2 * P:3 * P], ACT.Copy)
                ins.then_inc(hi_done, 1)

            def exponent(at, p_):
                for e in range(2):
                    head = NH * VW + 2 * p_ + e
                    act.wait_ge(biased, at.pair(p_) * 2 + (e + 1))
                    if e == 0:
                        wait(act, p_turned, at.pair(p_) - 1)
                    act.activation(p[p_ % 2][:, e, 0:at.grp.w], s_b[p_ % 3][:, e, 0:at.grp.w], ACT.Exp,
                                   bias=o[at.s][:, head:head + 1], scale=-1.0).then_inc(exp_done, 1)

            def copy_p(at, p_):
                g, chunks = at.pair(p_), at.grp.chunks
                act.wait_ge(p_turned, g + 1)
                wait(act, pv_done, g - 1)
                src = ps_p[:].rearrange("p (e j q) -> p e j q", e=2, j=2)
                if chunks == [P, P]:
                    act.activation(p_t[p_ % 2][:], src, ACT.Copy).then_inc(p_copied, 1)
                else:
                    for j, n in enumerate(chunks):
                        ins = act.activation(p_t[p_ % 2][0:n, :, j, :], src[0:n, :, j, :], ACT.Copy)
                    ins.then_inc(p_copied, 1)

            def prologue(at):
                act.wait_ge(gain_done, 1)
                act.wait_ge(cleared, 7)
                for p_ in range(TURN):
                    upper(at, p_)
                    if p_ >= TURN - EXP:
                        exponent(at, p_ - TURN + EXP)
                copy_p(at, 0)

            def tile(at, more):
                for p_ in range(PAIRS):
                    if at.ahead(p_ + EXP):
                        exponent(*at.ahead(p_ + EXP))
                    if at.ahead(p_ + TURN_P):
                        copy_p(*at.ahead(p_ + TURN_P))
                    if at.ahead(p_ + TURN):
                        upper(*at.ahead(p_ + TURN))

            def split_w(n):
                if n in split_at:
                    k_ = split_at.index(n)
                    act.wait_ge(w_in, 16 * KC)
                    act.activation(core.w_out_hi[:, k_, :], stage[k_], ACT.Copy).then_inc(w_hi_done, 1)

            runs(act, prologue, tile, split_w)

        @block.vector
        def _(dve):
            dve.wait_ge(table_in, 16 * 4)
            dve.tensor_scalar(gain[:], gain_q[:], gain_k[:], 1.0 / math.sqrt(HD), ALU.mult,
                              ALU.mult).then_inc(gain_done, 1)
            dve.wait_ge(gain_done, 1)
            dve.wait_ge(cleared, 3)
            for part in q_hi + q_lo:
                dve.tensor_copy(part[:], zeros[:]).then_inc(cleared, 1)
            dve.wait_ge(cleared, 7)

            def lower(at, p_):
                w, b = at.grp.w, p_ % 2
                dve.wait_ge(hi_done, at.pair(p_) + 1)
                if w == P:
                    dve.tensor_copy(q_all[b][HD:P, 1, :], ps_t[b][HD:P, 2 * P:3 * P]).then_inc(qk_copied, 1)
                    return
                for e in range(2):
                    rows = slice(HD * e, HD * (e + 1))
                    dve.tensor_tensor(q_lo[b][rows, e, :], ps_t[p_ % 2][rows, 2 * P:3 * P],
                                      q_hi[b][rows, e, :].bitcast(F32), ALU.subtract)
                dve.scalar_tensor_tensor(k_lo[b][:, 0:w], ps_t[p_ % 2][:, 0:w], gain[:], k_hi[b][:, 0:w].bitcast(F32),
                                         ALU.mult, ALU.subtract).then_inc(qk_copied, 1)

            def add_bias(at, p_):
                grp, s, b = at.grp, at.s, p_ % 2
                if p_ == 0 and not (isinstance(at.nr, int) and at.nr < 2):
                    dve.wait_ge(stored[s], (at.nr - s) * 8)
                for e in range(2):
                    head = 2 * p_ + e
                    dve.wait_ge(scored, at.pair(p_) * 2 + (e + 1))
                    wait(dve, exp_done, at.pair(p_) * 2 + (e - 5))
                    dve.sem_inc(waited, 1)
                    dve.tensor_tensor_reduce(s_b[p_ % 3][:, e, 0:grp.w], ps_s[head % 3][:, 0:grp.w],
                                             bias[:, DILS.index(grp.dil), head, grp.lo:grp.lo + grp.w], -1.0, -3 * NEG,
                                             ALU.add, ALU.min, o[s][:, NH * VW + head:NH * VW + head + 1]).then_inc(biased, 1)

            def copy_o(at, p_):
                b = p_ // 3
                dve.wait_ge(pv_done, at.pair(p_) + 1)
                dve.tensor_copy(o[at.s][:, b * 6 * VW:(b + 1) * 6 * VW], ps_o[b][:, 0:6 * VW]).then_inc(o_copied, 1)

            def prologue(at):
                lower(at, 0)
                dve.wait_ge(bias_in[0], 16)
                for p_ in range(1, TURN):
                    lower(at, p_)
                    add_bias(at, p_ - 1)
                for i in range(1, len(DILS)):
                    dve.wait_ge(bias_in[i], 16)

            def tile(at, more):
                for p_ in range(PAIRS):
                    if at.ahead(p_ + TURN):
                        lower(*at.ahead(p_ + TURN))
                    if at.ahead(p_ + SCORE):
                        add_bias(*at.ahead(p_ + SCORE))
                    if p_ % 3 == 2:
                        copy_o(at, p_)

            def split_w(n):
                if n in split_at:
                    k_ = split_at.index(n)
                    dve.wait_ge(w_hi_done, k_ + 1)
                    dve.tensor_tensor(core.w_out_lo[:, k_, :], stage[k_], core.w_out_hi[:, k_, :].bitcast(F32),
                                      ALU.subtract).then_inc(w_lo_done, 1)

            runs(dve, prologue, tile, split_w)



def combine(core):
    nc, io, dram = core.nc, core.io, core.dram
    S = lambda n: core.sem("out_" + n)
    rows_in, x_in, mix_done = [S("rows_in0"), S("rows_in1")], [S("x_in0"), S("x_in1")], S("mix_done")
    shift_done, exp_done, share_done, acc_done = S("shift_done"), S("exp_done"), S("share_done"), S("acc_done")
    t_done, hi_done, lo_done = S("t_done"), S("hi_done"), S("lo_done")
    mm_done, y_done, chain, stored = S("mm_done"), S("y_done"), S("chain"), [S("stored0"), S("stored1")]
    n_d = len(DILS)
    LOADS = n_d + 2
    LINKS = 11
    first = lambda t: isinstance(t, int) and t == 0
    early = lambda t: isinstance(t, int) and t < 2
    late = lambda t: isinstance(t, int) and t >= TILES - 2
    last = lambda t: isinstance(t, int) and t == TILES - 1

    def tiles(engine, step):
        step(0, 0)
        step(1, 1)
        with engine.Fori(1, TILES // 2 - 2) as it:
            step(it * 2, 0)
            step(it * 2 + 1, 1)
        for t in range(TILES - 4, TILES):
            step(t, t % 2)

    with ExitStack() as st:
        sb = lambda n, shape, dt=F32: core.sb(st, "out_" + n, shape, dt)
        w_hi, w_lo = core.w_out_hi, core.w_out_lo
        o = [sb(f"o{i}", [P, n_d, OROW]) for i in range(2)]
        gate = [sb(f"gate{i}", [P, D]) for i in range(2)]
        four = [sb(f"four{i}", [P, DF]) for i in range(2)]
        x = [sb(f"x{i}", [P, D]) for i in range(2)]
        least, shift, weight, part = (sb(n, [P, n_d, NH]) for n in ("least", "shift", "weight", "part"))
        total, inv = sb("total", [P, NH]), sb("inv", [P, NH])
        acc, term = sb("acc", [P, DA]), [sb(f"term{i}", [P, DA]) for i in range(2)]
        mix = [sb(f"mix{i}", [P, D]) for i in range(2)]
        m_hi = [sb(f"m_hi{i}", [P, KC, P], F32R) for i in range(2)]
        m_lo = [sb(f"m_lo{i}", [P, KC, P], F32R) for i in range(2)]
        y = [sb(f"y{i}", [P, D]) for i in range(2)]
        ps_t = [core.ps(st, f"out_ps_t{i}") for i in range(4)]
        ps_y = [core.ps(st, f"out_ps_y{i}") for i in range(4)]
        block = st.enter_context(nc.Block())

        @block.sync
        def _(sp):
            def load_rows(t, s):
                if not early(t):
                    sp.wait_ge(mix_done, t - 1)
                at = bass.ds(t * P, P)
                for i in range(n_d):
                    sp.dma_start(o[s][:, i, :], dram["o"][i, at, :]).then_inc(rows_in[s], 16)
                sp.dma_start(gate[s][:], dram["gate"][at, :]).then_inc(rows_in[s], 16)
                sp.dma_start(four[s][:], dram["four"][at, :]).then_inc(rows_in[s], 16)

            def load_x(t, s):
                sp.dma_start(x[s][:], io["x"][bass.ds(t * P, P), :]).then_inc(x_in[s], 16)

            load_rows(0, 0)
            load_rows(1, 1)
            load_x(0, 0)
            load_x(1, 1)
            load_rows(2, 0)

            def step(t, s):
                if not (isinstance(t, int) and t + 3 >= TILES):
                    load_rows(t + 3, 1 - s)
                sp.wait_ge(y_done, t * 2 + 2)
                sp.dma_start(io["y"][bass.ds(t * P, P), :], y[s][:]).then_inc(stored[s], 16)
                if not late(t):
                    load_x(t + 2, s)

            tiles(sp, step)
            for s in range(2):
                sp.wait_ge(stored[s], 16 * TILES // 2)

        @block.tensor
        def _(pe):
            def turn(t, s):
                pe.wait_ge(mix_done, t + 1)
                if not early(t):
                    pe.wait_ge(lo_done, t * 2 - 2)
                for j in range(2):
                    for k in range(4):
                        ins = pe.transpose(ps_t[2 * s + j][:, k * P:(k + 1) * P],
                                           mix[s][:, (4 * j + k) * P:(4 * j + k + 1) * P], core.ident[:])
                    ins.then_inc(t_done, 1)

            def step(t, s):
                pe.wait_ge(lo_done, t * 2 + 2)
                for c in range(2):
                    if not early(t):
                        pe.wait_ge(y_done, t * 2 + (c - 3))
                    for k in range(KC):
                        for n, (a, b) in enumerate(((m_hi, w_hi), (m_hi, w_lo), (m_lo, w_hi))):
                            ins = pe.matmul(ps_y[2 * s + c][:], a[s][:, k, :], b[:, k, c * BANK:(c + 1) * BANK],
                                            start=(k == 0 and n == 0), stop=(k == KC - 1 and n == 2))
                    ins.then_inc(mm_done, 1)
                    if c == 0 and not last(t):
                        turn(t + 1, 1 - s)

            turn(0, 0)
            tiles(pe, step)

        @block.scalar
        def _(act):
            def weights(t):
                act.wait_ge(shift_done, t + 1)
                act.activation(weight[:], shift[:], ACT.Exp).then_inc(exp_done, 1)

            def first_term(t, s):
                act.wait_ge(share_done, t + 1)
                for h in range(NH):
                    ins = act.activation(acc[:, h * HD:(h + 1) * HD], o[s][:, 0, h * VW:h * VW + HD], ACT.Copy,
                                         scale=part[:, 0, h:h + 1])
                ins.then_inc(acc_done, 1)

            def split(t, s):
                for j in range(2):
                    act.wait_ge(t_done, t * 2 + j + 1)
                    if j == 0 and not early(t):
                        act.wait_ge(mm_done, t * 2 - 2)
                    ins = act.activation(m_hi[s][:, 4 * j:4 * j + 4, :],
                                         ps_t[2 * s + j][:].rearrange("p (k c) -> p k c", k=4), ACT.Copy)
                    ins.then_inc(hi_done, 1)

            def step(t, s):
                if not late(t):
                    weights(t + 2)
                    first_term(t + 2, s)
                if not last(t):
                    split(t + 1, 1 - s)

            weights(0)
            first_term(0, 0)
            split(0, 0)
            weights(1)
            first_term(1, 1)
            tiles(act, step)

        @block.vector
        def _(dve):
            def mixed(t, s):
                links = t * LINKS
                at = [0]

                def link(ins):
                    at[0] += 1
                    ins.then_inc(chain, 1)
                    dve.wait_ge(chain, links + at[0])

                dve.wait_ge(rows_in[s], (t - s) * (8 * LOADS) + 16 * LOADS)
                low = o[s][:, :, NH * VW:]
                heads = o[s][:, :, 0:NH * VW].rearrange("p i (h w) -> p i h w", w=VW)
                link(dve.tensor_tensor(least[:, 0, :], low[:, 0, :], low[:, 1, :], ALU.min))
                link(dve.tensor_tensor(least[:, 0, :], least[:, 0, :], low[:, 2, :], ALU.min))
                dve.tensor_tensor(shift[:], least[:, 0:1, :].broadcast_to([P, n_d, NH]), low,
                                  ALU.subtract).then_inc(shift_done, 1)
                dve.wait_ge(exp_done, t + 1)
                link(dve.tensor_tensor(part[:], weight[:], heads[:, :, :, HD], ALU.mult))
                link(dve.tensor_tensor(total[:], part[:, 0, :], part[:, 1, :], ALU.add))
                link(dve.tensor_tensor(total[:], total[:], part[:, 2, :], ALU.add))
                link(dve.reciprocal(inv[:], total[:]))
                dve.tensor_tensor(part[:], weight[:], inv[:].rearrange("p (a h) -> p a h", a=1).broadcast_to([P, n_d, NH]),
                                  ALU.mult).then_inc(share_done, 1)
                dve.wait_ge(share_done, t + 1)
                spread = lambda i: part[:, i, :].rearrange("p (h w) -> p h w", w=1).broadcast_to([P, NH, HD])
                term_h = [b[:].rearrange("p (h w) -> p h w", w=HD) for b in term]
                if not early(t):
                    dve.wait_ge(t_done, t * 2 - 2)
                link(dve.tensor_tensor(mix[s][:, DA:], four[s][:], gate[s][:, DA:], ALU.mult))
                for i in range(1, n_d):
                    link(dve.tensor_tensor(term_h[i - 1], heads[:, i, :, 0:HD], spread(i), ALU.mult))
                link(dve.tensor_tensor(term[0][:], term[0][:], term[1][:], ALU.add))
                dve.wait_ge(acc_done, t + 1)
                link(dve.tensor_tensor(term[0][:], term[0][:], acc[:], ALU.add))
                dve.tensor_tensor(mix[s][:, 0:DA], term[0][:], gate[s][:, 0:DA], ALU.mult).then_inc(mix_done, 1)
                assert at[0] == LINKS

            def split(t, s):
                for j in range(2):
                    dve.wait_ge(hi_done, t * 2 + j + 1)
                    dve.tensor_tensor(m_lo[s][:, 4 * j:4 * j + 4, :],
                                      ps_t[2 * s + j][:].rearrange("p (k c) -> p k c", k=4),
                                      m_hi[s][:, 4 * j:4 * j + 4, :].bitcast(F32), ALU.subtract).then_inc(lo_done, 1)

            def add_x(t, s, c):
                dve.wait_ge(mm_done, t * 2 + (c + 1))
                if c == 0:
                    if not early(t):
                        dve.wait_ge(stored[s], (t - s) * 8)
                    dve.wait_ge(x_in[s], (t - s) * 8 + 16)
                cols = slice(c * BANK, (c + 1) * BANK)
                dve.tensor_tensor(y[s][:, cols], ps_y[2 * s + c][:], x[s][:, cols], ALU.add).then_inc(y_done, 1)

            def step(t, s):
                if not late(t):
                    mixed(t + 2, s)
                add_x(t, s, 0)
                if not last(t):
                    split(t + 1, 1 - s)
                add_x(t, s, 1)

            mixed(0, 0)
            split(0, 0)
            mixed(1, 1)
            tiles(dve, step)



def kernel(x_prompt, x_sample, norm_g, w_in, q_norm_g, k_norm_g, rel_bias, w_four, w_out):
    from concourse import bacc
    from concourse.bass_utils import run_bass_kernel_spmd

    nc = bacc.Bacc("TRN2", target_bir_lowering=False, num_devices=1)
    arrays = {"x": np.concatenate([np.asarray(x_prompt)[0], np.asarray(x_sample)[0]], axis=0),
              "norm_g": np.asarray(norm_g)[0], "w_in": np.asarray(w_in)[0], "q_norm_g": np.asarray(q_norm_g)[0],
              "k_norm_g": np.asarray(k_norm_g)[0], "rel_bias": np.asarray(rel_bias),
              "w_four": np.asarray(w_four)[0], "w_out": np.asarray(w_out)[0]}
    arrays.update(constants())
    io = {k: nc.dram_tensor(k, a.shape, mybir.dt.from_np(a.dtype), kind="ExternalInput").ap()
          for k, a in arrays.items()}
    io["y"] = nc.dram_tensor("y", (TOKENS, D), F32, kind="ExternalOutput").ap()
    build(nc, io)
    y = run_bass_kernel_spmd(nc, [arrays], core_ids=[0]).results[0]["y"]
    return y[None, :SEQS[0]], y[None, SEQS[0]:]
```
